# Optimizing a Trainium2 kernel written in Bass

```python
import jax, jax.numpy as jnp
from jax import lax
import numpy as np

D_MODEL = 1024
BATCH = 1
SEQ = 512
DEPTH = 1
DEC_BATCH = 8
DEC_SEQ = 1
PAST_LEN = 4096
PAGE_SIZE = 128

N_HEADS_A = 4
DK_A = 128
DV_A = 256
MLSTM_CHUNK = 128
D_B = 1024
N_GROUPS_B = 4
DG_B = D_B // N_GROUPS_B
CHUNK_B = 128
D_FF = 2816
CONV_W = 3
EPS = 1e-6
P_IN = 2 * N_HEADS_A * DK_A + 2 * N_HEADS_A * DV_A + 2 * N_HEADS_A + 2 * D_B + 2 * D_MODEL

kernel_name = "hybrid_mlstm_gmlp_convffn_step"

def rmsnorm(x, g):
    xf = x.astype(jnp.float32)
    r = lax.rsqrt(jnp.mean(xf * xf, axis=-1, keepdims=True) + EPS)
    return (xf * r * g.astype(jnp.float32)).astype(x.dtype)

def split_in(z):
    sizes = (N_HEADS_A * DK_A, N_HEADS_A * DK_A, N_HEADS_A * DV_A, N_HEADS_A * DV_A,
             N_HEADS_A, N_HEADS_A, D_B, D_B, D_MODEL, D_MODEL)
    idx = np.cumsum(sizes)[:-1].tolist()
    return jnp.split(z, idx, axis=-1)

def mlstm_chunk(carry, q, k, v, ig, lf):
    C, n, m = carry
    L = q.shape[-2]
    causal = jnp.tril(jnp.ones((L, L), dtype=bool))
    b = jnp.cumsum(lf, axis=-1)
    logD = b[..., :, None] - b[..., None, :] + ig[..., None, :]
    logD = jnp.where(causal, logD, -jnp.inf)
    inter = b + m[..., None]
    m_t = jnp.maximum(inter, jnp.max(logD, axis=-1))
    Dmat = jnp.exp(logD - m_t[..., None])
    w_inter = jnp.exp(inter - m_t)
    s = jnp.einsum('nhtk,nhsk->nhts', q, k) * Dmat
    num = jnp.einsum('nhts,nhsv->nhtv', s, v) + w_inter[..., None] * jnp.einsum('nhvk,nhtk->nhtv', C, q)
    den = jnp.sum(s, axis=-1) + w_inter * jnp.einsum('nhk,nhtk->nht', n, q)
    h = num / jnp.maximum(jnp.abs(den), jnp.exp(-m_t))[..., None]
    m_new = m_t[..., -1]
    w_last = Dmat[..., -1, :]
    decay = w_inter[..., -1]
    C_new = decay[..., None, None] * C + jnp.einsum('nhs,nhsv,nhsk->nhvk', w_last, v, k)
    n_new = decay[..., None] * n + jnp.einsum('nhs,nhsk->nhk', w_last, k)
    return (C_new, n_new, m_new), h

def mlstm_branch(q, k, v, ig, lf, C, n, m):
    N, S = q.shape[0], q.shape[1]
    L = min(S, MLSTM_CHUNK)
    nc = S // L

    def to_chunks(t):
        t = t.astype(jnp.float32).reshape((N, nc, L) + t.shape[2:])
        t = jnp.moveaxis(t, 1, 0)
        return jnp.swapaxes(t, 2, 3)

    xs = (to_chunks(q), to_chunks(k), to_chunks(v), to_chunks(ig), to_chunks(lf))

    def step(carry, xc):
        return mlstm_chunk(carry, *xc)

    init = (C.astype(jnp.float32), n.astype(jnp.float32), m.astype(jnp.float32))
    (C, n, m), h = lax.scan(step, init, xs)
    h = jnp.swapaxes(jnp.moveaxis(h, 0, 1), 2, 3).reshape(N, S, N_HEADS_A * DV_A)
    return h, C, n, m

def spatial_gate(u, vn, w_s, b_s):
    N, S, _ = vn.shape
    L = min(S, CHUNK_B)
    nc = S // L
    vg = vn.reshape(N, nc, L, N_GROUPS_B, DG_B)
    causal = jnp.tril(jnp.ones((L, L), dtype=bool))
    w = jnp.where(causal, w_s[:, :L, :L], 0.0).astype(vn.dtype)
    mixed = jnp.einsum('gts,ncsgd->nctgd', w, vg) + b_s[:, :L].T[None, None, :, :, None].astype(vn.dtype)
    return u * mixed.reshape(N, S, D_B)

def layer(x, C, n, m, conv_buf, w_in, b_ig, b_fg, g1, g_v, w_s, b_s, w_a, w_b, w_o, g2, w_up, c_w, c_b, w_down):
    N, S, _ = x.shape
    xn = rmsnorm(x, g1)
    z = xn @ w_in
    q, k, v, o, ig, fg, u, vb, ga, gb = split_in(z)
    q = q.reshape(N, S, N_HEADS_A, DK_A)
    k = k.reshape(N, S, N_HEADS_A, DK_A) * (DK_A ** -0.5)
    v = v.reshape(N, S, N_HEADS_A, DV_A)
    ig = ig.astype(jnp.float32) + b_ig.astype(jnp.float32)
    lf = jax.nn.log_sigmoid(fg.astype(jnp.float32) + b_fg.astype(jnp.float32))
    h, C, n, m = mlstm_branch(q, k, v, ig, lf, C, n, m)
    y_a = (jax.nn.sigmoid(o) * h.astype(x.dtype)) @ w_a
    u = jax.nn.gelu(u)
    vn = rmsnorm(jax.nn.gelu(vb), g_v)
    y_b = spatial_gate(u, vn, w_s, b_s) @ w_b
    x = x + (jax.nn.sigmoid(ga) * y_a + jax.nn.sigmoid(gb) * y_b) @ w_o
    xn = rmsnorm(x, g2)
    up = xn @ w_up
    pad = jnp.concatenate([conv_buf.astype(up.dtype), up], axis=1)
    conv = c_b + c_w[0] * pad[:, 0:S]
    for j in range(1, CONV_W):
        conv = conv + c_w[j] * pad[:, j:j + S]
    a, gval = jnp.split(conv, 2, axis=-1)
    x = x + (jax.nn.silu(a) * gval) @ w_down
    return x, C, n, m, pad[:, -(CONV_W - 1):], vn

def setup_inputs(seed: int = 0) -> dict:
    key = jax.random.key(seed)
    ks = jax.random.split(key, 24)
    nrm = jax.random.normal
    f32 = jnp.float32
    inp = {}
    inp['x_prompt'] = nrm(ks[0], (BATCH, SEQ, D_MODEL), f32)
    inp['x_sample'] = nrm(ks[1], (DEC_BATCH, DEC_SEQ, D_MODEL), f32)
    inp['state_mlstm_C'] = 0.5 * nrm(ks[2], (DEPTH, DEC_BATCH, N_HEADS_A, DV_A, DK_A), f32)
    inp['state_mlstm_n'] = 0.5 * nrm(ks[3], (DEPTH, DEC_BATCH, N_HEADS_A, DK_A), f32)
    inp['state_mlstm_m'] = nrm(ks[4], (DEPTH, DEC_BATCH, N_HEADS_A), f32)
    inp['state_ffn_conv'] = nrm(ks[5], (DEPTH, DEC_BATCH, CONV_W - 1, 2 * D_FF), f32)
    inp['w_in'] = nrm(ks[6], (DEPTH, D_MODEL, P_IN), f32) * D_MODEL ** -0.5
    inp['b_igate'] = -1.0 + 0.1 * nrm(ks[7], (DEPTH, N_HEADS_A), f32)
    inp['b_fgate'] = 3.0 + 0.1 * nrm(ks[8], (DEPTH, N_HEADS_A), f32)
    inp['g_norm1'] = 1.0 + 0.05 * nrm(ks[9], (DEPTH, D_MODEL), f32)
    inp['g_vnorm'] = 1.0 + 0.05 * nrm(ks[10], (DEPTH, D_B), f32)
    inp['w_spatial'] = 0.5 * nrm(ks[11], (DEPTH, N_GROUPS_B, CHUNK_B, CHUNK_B), f32) * CHUNK_B ** -0.5
    inp['b_spatial'] = 1.0 + 0.1 * nrm(ks[12], (DEPTH, N_GROUPS_B, CHUNK_B), f32)
    inp['w_branch_a'] = nrm(ks[13], (DEPTH, N_HEADS_A * DV_A, D_MODEL), f32) * (N_HEADS_A * DV_A) ** -0.5
    inp['w_branch_b'] = nrm(ks[14], (DEPTH, D_B, D_MODEL), f32) * D_B ** -0.5
    inp['w_out'] = nrm(ks[15], (DEPTH, D_MODEL, D_MODEL), f32) * D_MODEL ** -0.5
    inp['g_norm2'] = 1.0 + 0.05 * nrm(ks[16], (DEPTH, D_MODEL), f32)
    inp['w_up'] = nrm(ks[17], (DEPTH, D_MODEL, 2 * D_FF), f32) * D_MODEL ** -0.5
    inp['conv_w'] = nrm(ks[18], (DEPTH, CONV_W, 2 * D_FF), f32) * CONV_W ** -0.5
    inp['conv_b'] = 0.02 * nrm(ks[19], (DEPTH, 2 * D_FF), f32)
    inp['w_down'] = nrm(ks[20], (DEPTH, D_FF, D_MODEL), f32) * D_FF ** -0.5
    inp['g_final'] = 1.0 + 0.05 * nrm(ks[21], (D_MODEL,), f32)
    return inp

def reference(x_prompt, x_sample, state_mlstm_C, state_mlstm_n, state_mlstm_m, state_ffn_conv,
              w_in, b_igate, b_fgate, g_norm1, g_vnorm, w_spatial, b_spatial, w_branch_a, w_branch_b,
              w_out, g_norm2, w_up, conv_w, conv_b, w_down, g_final):
    nb = x_prompt.shape[0]
    xp, xs = x_prompt, x_sample
    Cp_l, np_l, mp_l, cp_l = [], [], [], []
    Cs_l, ns_l, ms_l, cs_l, vs_l = [], [], [], [], []
    for l in range(DEPTH):
        params = (w_in[l], b_igate[l], b_fgate[l], g_norm1[l], g_vnorm[l], w_spatial[l], b_spatial[l],
                  w_branch_a[l], w_branch_b[l], w_out[l], g_norm2[l], w_up[l], conv_w[l], conv_b[l], w_down[l])
        C0 = jnp.zeros((nb, N_HEADS_A, DV_A, DK_A), jnp.float32)
        n0 = jnp.zeros((nb, N_HEADS_A, DK_A), jnp.float32)
        m0 = jnp.zeros((nb, N_HEADS_A), jnp.float32)
        cb0 = jnp.zeros((nb, CONV_W - 1, 2 * D_FF), xp.dtype)
        xp, Cp, npr, mp, cp, _ = layer(xp, C0, n0, m0, cb0, *params)
        xs, Cs, ns, ms, cs, vs = layer(xs, state_mlstm_C[l], state_mlstm_n[l], state_mlstm_m[l],
                                       state_ffn_conv[l], *params)
        Cp_l.append(Cp); np_l.append(npr); mp_l.append(mp); cp_l.append(cp)
        Cs_l.append(Cs); ns_l.append(ns); ms_l.append(ms); cs_l.append(cs); vs_l.append(vs)
    y_prompt = rmsnorm(xp, g_final)
    y_sample = rmsnorm(xs, g_final)
    return (y_prompt, y_sample,
            jnp.stack(Cp_l), jnp.stack(np_l), jnp.stack(mp_l), jnp.stack(cp_l),
            jnp.stack(Cs_l), jnp.stack(ns_l), jnp.stack(ms_l), jnp.stack(cs_l), jnp.stack(vs_l))


_drawn_inputs = setup_inputs


def setup_inputs(seed=0):
    import zlib

    import numpy as np

    out = dict(_drawn_inputs(seed))
    spreads = {}
    factors = {'conv_b': 4.364}
    for name, (base, spread) in spreads.items():
        noise = np.random.default_rng([zlib.crc32(name.encode()), seed]).standard_normal(out[name].shape)
        drawn = base * np.exp(spread * noise) if base else spread * noise
        out[name] = __import__('jax').numpy.asarray(drawn.astype(out[name].dtype))
    for name, factor in factors.items():
        out[name] = (out[name] * factor).astype(out[name].dtype)
    return out
```

```python
from contextlib import ExitStack

import concourse.bass as bass
from concourse import mybir

F32 = mybir.dt.float32
F32R = mybir.dt.float32r
ALU = mybir.AluOpType
ACT = mybir.ActivationFunctionType
AX_X = mybir.AxisListType.X

P = 128
D_MODEL, SEQ, NB = 1024, 512, 8
NH, DK, DV = 4, 128, 256
NG, D_FF, CONV_W = 4, 2816, 3
EPS = 1e-6
TOK = SEQ + NB
HALF = TOK // 2
KT = D_MODEL // P
NC = SEQ // P
FT = D_FF // P
DVA = DV + 1
BIG = -3.0e38

S_GATE = 0
S_VB = S_GATE + 1
S_Q = S_VB + 8
S_U = S_Q + NH
S_K = S_U + 8
S_V = S_K + NH
S_O = S_V + 8
S_BY = S_O + 8
S_AY = S_BY + 16
S_WO = S_AY + 16
S_UP = S_WO + 8
S_DN = S_UP + 2 * FT
DN_CUTS = (0, 8, 15, 22)
N_SLOTS = S_DN + 3 * KT

B_VB, B_SP, B_K, B_V, B_UNIT = 0, 8, 16, 20, 28
ROW = 2 * NH * DK + 4 * NH


class At:

    def __init__(self, c, i=None, s=0):
        self.c, self.i, self.s = c, i, s

    def __call__(self, extra=0):
        return self.c + extra if self.i is None else self.i * self.s + (self.c + extra)

    def half(self, extra=0):
        return self.c // 2 + extra if self.i is None else self.i * (self.s // 2) + (self.c // 2 + extra)

    def plus(self, k):
        return At(self.c + k, self.i, self.s)


def hybrid_layer(nc, ins, outs):
    with ExitStack() as ctx:
        base = nc.sbuf_base + 64 - nc.sbuf_base % 64
        ARENA = 190528
        fence = ctx.enter_context(nc.sbuf_tensor("arena", [P, (ARENA + 64) // 4], F32))
        assert fence is not None

        def at(name, shape, offset, dt=F32):
            return nc.alloc_sbuf_tensor_at(name, shape, dt, offset=base + offset)

        def sb(name, shape, dt=F32):
            return ctx.enter_context(nc.sbuf_tensor(name, shape, dt))

        def sem(name):
            return ctx.enter_context(nc.semaphore(name))

        XB = KT * TOK * 4
        xh = at("xh", [P, KT, TOK], 0, F32R)
        xl = at("xl", [P, KT, TOK], XB, F32R)
        x2h = at("x2h", [P, KT, TOK], 0, F32R)
        x2l = at("x2l", [P, KT, TOK], XB, F32R)
        xg = at("xg", [P, KT, TOK], 0)
        y = at("y", [P, KT, TOK], XB)
        hbh = at("hbh", [P, KT, TOK], 2 * XB, F32R)
        hbl = at("hbl", [P, KT, TOK], 3 * XB, F32R)
        mh = at("mh", [P, KT, TOK], 2 * XB, F32R)
        ml = at("ml", [P, KT, TOK], 3 * XB, F32R)
        actl = at("actl", [P, FT, TOK], 2 * XB, F32R)
        g_tok = at("g_tok", [P, NC, D_MODEL], 4 * XB)
        gvrow = at("gvrow", [P, D_MODEL], 5 * XB)
        nmx = at("nmx", [NH, NH, SEQ], 5 * XB + 4096)
        d_arg = at("d_arg", [P, SEQ], 5 * XB + 12288)
        d_exp = at("d_exp", [P, SEQ], 5 * XB + 14336)
        bc = at("bc", [P, 2, ROW], 4 * XB)
        srows = at("srows", [NB, ROW], 4 * XB + 8320)
        tq = [at(f"tq{t}", [P, KT, DK], 4 * XB + 8320 + 4160 * t) for t in range(2)]
        n_s = at("n_s", [NB, NH * DK], 4 * XB + 12480)
        n_t = at("n_t", [NB, NH * DK], 4 * XB + 14528)
        hah = at("hah", [P, KT, TOK], 4 * XB, F32R)
        hal = at("hal", [P, KT, TOK], 5 * XB, F32R)
        so = at("so", [P, KT, TOK], 5 * XB)
        F0 = 79040
        cst = at("cst", [P, 2 * FT, 2, NB], F0)
        cwb = at("cwb", [P, 2 * FT, 4], F0 + 2816)
        sconv = at("sconv", [P, 2 * FT, NB], F0 + 3520)
        nconv = at("nconv", [P, 2 * FT, 2 + NB], F0 + 4928)
        up = [at(f"up{t}", [P, 2 + TOK], F0 + 6688 + 2112 * t) for t in range(2)]
        conv = [at(f"conv{t}", [P, TOK], F0 + 10912 + 2080 * t) for t in range(2)]
        silu = at("silu", [P, TOK], F0 + 15072)
        rbc2 = at("rbc2", [P, TOK], F0 + 17152)
        sct = at("sct", [P, 2 * FT, NB], F0 + 6688)
        assert F0 + 19232 <= 6 * XB
        M0 = 6 * XB
        x0 = at("x0", [P, KT, TOK], M0)
        ig = at("ig", [NH, TOK], M0)
        fg = at("fg", [NH, TOK], M0 + 2080)
        lf = at("lf", [NH, TOK], M0 + 4160)
        bcum = at("bcum", [NH, SEQ], M0 + 6240)
        mmax = at("mmax", [NH, SEQ], M0 + 8288)
        g3 = at("g3", [P, SEQ], M0 + 10336)
        lfe = at("lfe", [NH, TOK], M0 + 12384)
        c_ring = at("c_ring", [P, 4, KT, DK], M0)
        merged = at("merged", [P, KT, TOK], M0)
        x1 = at("x1", [P, KT, TOK], M0)
        Q0 = 7 * XB
        qT = at("qT", [P, NH, TOK], Q0)
        k_tok = at("k_tok", [P, NC, NH, DK], Q0 + 8320)
        v_tok = at("v_tok", [P, NC, NH, DVA], Q0 + 16512)
        sd = at("sd", [P, NH, NC, P], Q0 + 32960)
        assert Q0 + 41152 <= 165952
        xres = at("xres", [P, KT, TOK], Q0)
        acth = at("acth", [P, FT, TOK], Q0, F32R)
        R0 = 165952
        raw = [at(f"raw{t}", [P, KT * P], R0 + 4096 * t) for t in range(2)]
        whi = [at(f"whi{t}", [P, KT * P], R0 + 8192 + 4096 * t, F32R) for t in range(2)]
        wlo = [at(f"wlo{t}", [P, KT * P], R0 + 16384 + 4096 * t, F32R) for t in range(2)]
        assert R0 + 24576 == ARENA
        ident = sb("ident", [P, P])
        ones = sb("ones", [P, P])
        maskmin = sb("maskmin", [P, P])
        sp_at = nc.sbuf_base + 64 - nc.sbuf_base % 64
        sp_place = sb("sp_place", [P, 4160 // 4])
        assert sp_place is not None
        ws = nc.alloc_sbuf_tensor_at("ws", [P, NG, P], F32, offset=sp_at)
        bs = nc.alloc_sbuf_tensor_at("bs", [P, NG, P], F32, offset=sp_at + 2048)
        state = sb("state", [P, NH, DVA])
        ftmp = [sb(f"ftmp{t}", [P, TOK]) for t in range(2)]
        stage_at = nc.sbuf_base + 64 - nc.sbuf_base % 64
        stage = sb("stage", [P, 5184 // 4])
        assert stage is not None

        def st(name, shape, offset):
            return nc.alloc_sbuf_tensor_at(name, shape, F32, offset=stage_at + offset)

        sq = [st(f"sq{t}", [P, TOK], 2080 * t) for t in range(2)]
        acct = st("acct", [P, NC, P], 0)
        sqt = st("sqt", [P, NC, P], 2048)
        vst = [st(f"vst{t}", [P, NC, P], 2048 * t) for t in range(2)]
        wq = st("wq", [P, SEQ], 0)
        kv = st("kv", [P, KT, DK], 0)
        hn = [st(f"hn{t}", [P, DV], 1024 * t) for t in range(2)]

        def spare(name, offset):
            return nc.alloc_sbuf_tensor_at(name, [P, P], F32, offset=sp_at + offset)

        sds = [spare(f"sds{t}", 512 * t) for t in range(2)]
        qs = [spare(f"qs{t}", 1024 + 512 * t) for t in range(2)]
        kw = [spare(f"kw{t}", 2048 + 512 * t) for t in range(2)]
        acc = st("acc", [P, TOK], 0)
        sqa = st("sqa", [P, TOK], 2080)

        gains = sb("gains", [P, 4, KT])
        w00 = sb("w00", [P, NG])
        gb = sb("gb", [NH, 2])
        eps = sb("eps", [P, 1])
        mrun = sb("mrun", [NH, NC + 1])
        ni4 = sb("ni4", [NH, NH])
        dm = sb("dm", [NH, 2, NC, NH])
        gcol = sb("gcol", [P, NC, NH])
        wlast = sb("wlast", [P, NC, NH])
        enm = sb("enm", [P, NC, NH])
        decay = sb("decay", [P, NC, NH])
        mpb = sb("mpb", [P, NC, NH])
        rv = sb("rv", [P, NC + NB])
        gvs = sb("gvs", [P, KT, NB])
        ssq = sb("ssq", [P, KT, NB])
        mixs = sb("mixs", [P, KT, NB])
        us = sb("us", [P, KT, NB])
        ks = sb("ks", [P, NH, NB])
        vs = sb("vs", [P, NB, KT])
        hs = sb("hs", [P, KT, NB])
        wv = [sb(f"wv{t}", [P, KT]) for t in range(2)]
        cq = sb("cq", [P, 3, KT])
        srt = sb("srt", [NB, 12, NH])
        nd = sb("nd", [P, 2, 3])

        out_ps = [ctx.enter_context(nc.psum_tensor(f"out{t}", [P, 2, 512], F32)) for t in range(2)]
        trp = [ctx.enter_context(nc.psum_tensor(f"trp{t}", [P, NC, P], F32)) for t in range(2)]
        aux = ctx.enter_context(nc.psum_tensor("aux", [P, 2, 512], F32))
        scratch = nc.dram_tensor("scratch", (NB, ROW), F32).ap()

        s_x = [sem(f"x_loaded{k}") for k in range(KT)]
        s_const = sem("consts_loaded")
        s_cp = sem("spatial_consts_loaded")
        s_ws = sem("spatial_weights_loaded")
        s_ss = sem("sample_states_loaded")
        s_init = sem("consts_made")
        s_tri = sem("triangles_made")
        s_sq = sem("square_ready")
        s_ssk = sem("square_summed")
        s_std = sem("std_ready")
        s_xr = sem("x_scaled")
        s_xh = sem("x_hi")
        s_xn = sem("x_lo")
        w_loaded = [sem(f"w_loaded{t}") for t in range(2)]
        w_hi = sem("w_hi")
        w_lo = sem("w_lo")
        done = sem("slots_done")
        evac = [sem(f"bank_emptied{t}") for t in range(2)]
        tr_done = sem("transposed")
        tre = [sem(f"tr_emptied{t}") for t in range(2)]
        s_vss = sem("v_squares_summed")
        s_vsr = sem("v_square_sums_ready")
        s_rv = sem("v_norm_std")
        s_ssm = sem("v_sample_sums")
        s_vst = sem("v_staged")
        s_hbp = sem("hb_product")
        s_hbh = sem("hb_hi")
        s_hbl = sem("hb_lo")
        s_ln = sem("softplus_ready")
        s_grow = sem("gate_rows")
        s_gcd = sem("gate_columns_done")
        s_gcol = sem("gate_columns")
        s_darg = sem("decay_exponents")
        s_wq = sem("inter_weights")
        s_de = sem("decay_matrix")
        s_auxu = sem("scores_used")
        s_rowd = sem("sample_rows_done")
        s_srow = sem("sample_rows")
        s_sg = sem("sample_gates")
        s_sge = sem("sample_gate_exps")
        s_srd = sem("sample_row_complete")
        s_scr = sem("scratch_written")
        s_bc = [sem(f"row_loaded{t}") for t in range(2)]
        s_cl = [sem(f"C_loaded{t}") for t in range(4)]
        s_cs = [sem(f"C_stored{t}") for t in range(4)]
        s_nst = sem("n_sample_stored")
        s_tq = sem("C_times_q")
        s_wv = sem("value_weights")
        s_kv = sem("kv_products")
        s_cn = sem("C_updated")
        s_stg = sem("unit_staged")
        s_num = sem("unit_numerator")
        s_unit = sem("unit_products_done")
        s_st = sem("state_ready")
        s_rd = sem("unit_denominator")
        s_ht = sem("unit_transposed")
        s_p = sem("ha_product")
        s_hah = sem("ha_hi")
        s_hal = sem("ha_lo")
        s_ms = sem("merged_sum")
        s_mh = sem("merged_hi")
        s_m = sem("merged_lo")
        s_xres = sem("residual_loaded")
        s_x1 = sem("x1_ready")
        s_x2h = sem("x2_hi")
        s_x2 = sem("x2_lo")
        s_acc = sem("norm2_sums")
        s_ss2 = sem("norm2_broadcast")
        s_std2 = sem("norm2_std")
        s_ffl = sem("ffn_consts_loaded")
        s_scv = sem("sample_conv_ready")
        s_up = sem("up_scaled")
        s_tap = sem("tap2_ready")
        s_cv = sem("conv_ready")
        s_sil = sem("silu_ready")
        s_pr = sem("hidden_product")
        s_ah = sem("hidden_hi")
        s_al = sem("hidden_lo")
        s_nc = sem("conv_rows_kept")
        s_x2f = sem("result_ready")
        s_sqf = sem("result_squared")
        s_accf = sem("final_sums")
        s_ssf = sem("final_broadcast")
        s_stdf = sem("final_std")
        s_rf = sem("final_scale")
        s_y = sem("y_dve")
        s_yp = sem("y_pool")
        s_out = sem("outputs_stored")
        s_yout = sem("y_stored")
        s_mp = sem("memory_prepared")

        def evacuated(eng, n):
            eng.wait_ge(evac[n.c % 2], n.half(2))

        block = ctx.enter_context(nc.Block())

        @block.sync
        def _(sp):
            def load(n, src, width=KT * P):
                p = n.c % 2
                if n.c >= 2:
                    sp.wait_ge(w_lo, n(-1))
                sp.dma_start(raw[p][:, 0:width], src).then_inc(w_loaded[p], 16)

            wp = ins["w_slots"]
            for n in range(2):
                load(At(n), wp[n])
            pairs = (S_DN - 3) // 2
            with sp.Fori(0, pairs) as i:
                for t in range(2):
                    n = At(2 + t, i, 2)
                    load(n, wp[n()])
            for n in range(2 + 2 * pairs, S_DN):
                load(At(n), wp[n])
            with sp.Fori(0, KT // 2) as i:
                for s in range(6):
                    a, b = DN_CUTS[s % 3], DN_CUTS[s % 3 + 1]
                    load(At(S_DN + s, i, 6), ins["w_dn"][i * 2 + s // 3, :, a * P:b * P], (b - a) * P)
            for j in (0, 1, 5, 2, 3, 6, 4, 7):
                if j < 5:
                    sp.wait_ge(s_y, j + 1)
                else:
                    sp.wait_ge(s_yp, j - 4)
                sp.dma_start(outs["y"][:, j, :], y[:, j, :]).then_inc(s_yout, 16)
            sp.wait_ge(s_yout, 16 * KT)

        @block.scalar
        def _(act):
            def A(out, in_, func=ACT.Copy, **kw_):
                return act.activation(out, in_, func, **kw_)

            def split(n, width=KT * P):
                p = n.c % 2
                act.wait_ge(w_loaded[p], n.half(1) * 16)
                if n.c >= 2:
                    act.wait_ge(done, n())
                A(whi[p][:, 0:width], raw[p][:, 0:width]).then_inc(w_hi, 1)

            def ready(n):
                act.wait_ge(done, n(2))

            def apart():
                act.wait_ge(done, 1)

            def both(t):
                return t.rearrange("p (a b) -> p a b", a=2)

            def out2(n):
                return out_ps[n.c % 2][:, :, 0:HALF]

            def smp(n):
                return out_ps[n.c % 2][:, 1, HALF - NB:HALF]

            for k in range(KT):
                act.dma_start(x0[:, k, :], ins["xT"][k]).then_inc(s_x[k], 16)
            act.dma_start(gains[:, :, :], ins["gains"]).then_inc(s_const, 16)
            act.dma_start(gb[:, :], ins["gate_b"]).then_inc(s_const, 16)
            for k in range(KT):
                act.wait_ge(s_x[k], 16)
                if k >= 2:
                    act.wait_ge(s_ssk, k - 1)
                A(sq[k % 2][:, :], x0[:, k, :], ACT.Square).then_inc(s_sq, 1)
            split(At(0))
            act.wait_ge(done, 1)
            act.wait_ge(s_init, 1)
            A(both(ftmp[0][:, :]), aux[:, :, 0:HALF], ACT.Sqrt, bias=eps[:, :], scale=1.0 / D_MODEL).then_inc(s_std, 1)
            split(At(1))
            act.wait_ge(s_const, 32)
            for k in range(KT):
                act.wait_ge(s_xr, k + 1)
                A(xh[:, k, :], x0[:, k, :], scale=gains[:, 0, k:k + 1]).then_inc(s_xh, 1)

            n = At(S_GATE)
            split(n.plus(2))
            ready(n)
            act.wait_ge(s_mp, 1)
            A(both(ig[:, :]), out_ps[0][0:NH, :, 0:HALF])
            A(both(fg[:, :]), out_ps[0][32:32 + NH, :, 0:HALF]).then_inc(evac[0], 1)

            def vb_step(i, t, first=False):
                n = At(S_VB + t, i, 2)
                j = i * 2 + t
                if first and t == 0:
                    act.drain()
                    A(lfe[:, :], fg[:, :], ACT.Abs, bias=gb[:, 1:2])
                    act.drain()
                    A(lfe[:, :], lfe[:, :], ACT.Exp, scale=-1.0)
                    act.drain()
                    A(lfe[:, :], lfe[:, :], ACT.Ln, bias=ones[0:NH, 0:1]).then_inc(s_ln, 1)
                split(n.plus(2))
                apart()
                ready(n)
                if not first:
                    act.wait_ge(tr_done, n(-2))
                A(gvs[:, j, :], smp(n), ACT.Gelu_apprx_tanh)
                A(both(ftmp[t][:, :]), out2(n), ACT.Gelu_apprx_tanh).then_inc(evac[n.c % 2], 1)

            for t in range(2):
                vb_step(0, t, True)
            with act.Fori(1, 4) as i:
                for t in range(2):
                    vb_step(i, t)

            def q_step(j):
                n = At(S_Q + j)
                if j == 2:
                    act.wait_ge(s_vsr, 1)
                    A(rv[:, :], rv[:, :], ACT.Sqrt, bias=eps[:, :], scale=1.0 / D_MODEL).then_inc(s_rv, 1)
                split(n.plus(2))
                ready(n)
                A(both(qT[:, j, :]), out2(n)).then_inc(evac[n.c % 2], 1)

            for j in range(NH):
                q_step(j)

            def u_step(i, t, first=False):
                n = At(S_U + t, i, 2)
                j = i * 2 + t
                split(n.plus(2))
                apart()
                ready(n)
                if first:
                    act.wait_ge(tr_done, B_VB + 7 + t)
                else:
                    act.wait_ge(s_hbl, i * 2 + (t - 1))
                A(us[:, j, :], smp(n), ACT.Gelu_apprx_tanh)
                A(both(ftmp[t][:, :]), out2(n), ACT.Gelu_apprx_tanh).then_inc(evac[n.c % 2], 1)
                apart()
                act.wait_ge(s_hbp, i * 2 + (t + 1))
                A(hbh[:, j, 0:SEQ], ftmp[t][:, 0:SEQ]).then_inc(s_hbh, 1)

            for t in range(2):
                u_step(0, t, True)
            with act.Fori(1, 4) as i:
                for t in range(2):
                    u_step(i, t)

            act.wait_ge(s_gcd, 1)
            A(gcol[:, :, :], aux[:, 0, :].rearrange("p (c t) -> p c t", c=NC)[:, :, 0:NH])
            A(wlast[:, :, :], aux[:, 0, :].rearrange("p (c t) -> p c t", c=NC)[:, :, 32:32 + NH], ACT.Exp)
            A(enm[:, :, :], aux[:, 0, :].rearrange("p (c t) -> p c t", c=NC)[:, :, 64:64 + NH], ACT.Exp)
            A(decay[:, :, :], aux[:, 1, 0:16].rearrange("p (c h) -> p c h", c=NC), ACT.Exp)
            A(mpb[:, :, :], aux[:, 1, 16:32].rearrange("p (c h) -> p c h", c=NC))
            A(srt[:, 0:2, :], aux[0:NB, 1, 64:72].rearrange("p (c h) -> p c h", c=2)).then_inc(s_gcol, 1)
            act.wait_ge(s_hbp, 9)
            A(hbh[:, :, SEQ:TOK], us[:, :, :]).then_inc(s_hbh, 1)

            def k_side(h):
                act.wait_ge(s_darg, h + 1)
                A(d_exp[:, :], d_arg[:, :], ACT.Exp).then_inc(s_de, 1)
                for c in range(NC):
                    a = A(wq[:, c * P:(c + 1) * P], aux[:, 1, c * P:(c + 1) * P], ACT.Exp, bias=mpb[:, c, h:h + 1])
                a.then_inc(s_wq, 1)
                A(k_tok[:, :, h, :], trp[h % 2][:, :, :]).then_inc(tre[h % 2], 1)

            for h in range(NH):
                n = At(S_K + h)
                if h >= 1:
                    k_side(h - 1)
                split(n.plus(2))
                ready(n)
                if h < 2:
                    act.wait_ge(s_hbl, 9)
                else:
                    act.wait_ge(tr_done, B_K + h - 1)
                A(ks[:, h, :], smp(n), scale=DK ** -0.5)
                A(both(ftmp[h % 2][:, :]), out2(n), scale=DK ** -0.5).then_inc(evac[n.c % 2], 1)

            def v_side(i, t):
                b = At(B_V + t, i, 2)
                apart()
                act.wait_ge(tr_done, b(1))
                A(v_tok[:, :, i, t * P:(t + 1) * P], trp[t][:, :, :]).then_inc(tre[t], 1)

            def v_step(i, t, first=False):
                n = At(S_V + t, i, 2)
                if first and t == 0:
                    k_side(NH - 1)
                else:
                    v_side(i - 1 + t, 1 - t)
                split(n.plus(2))
                apart()
                ready(n)
                act.wait_ge(tr_done, At(B_V + t, i, 2)(-1))
                A(vs[:, :, i * 2 + t], smp(n))
                A(both(ftmp[t][:, :]), out2(n)).then_inc(evac[n.c % 2], 1)

            for t in range(2):
                v_step(0, t, True)
            act.wait_ge(s_rowd, 1)
            A(srows[:, 0:512], aux[0:NB, 0, :])
            A(srows[:, 512:1024], aux[0:NB, 1, :]).then_inc(s_srow, 1)
            with act.Fori(1, 4) as i:
                for t in range(2):
                    v_step(i, t)
            v_side(3, 1)
            act.wait_ge(s_sg, 1)
            A(srt[:, 4:7, :], srt[:, 4:7, :], ACT.Exp).then_inc(s_sge, 1)

            def o_step(i, t):
                n = At(S_O + t, i, 4)
                act.wait_ge(s_wv, i * 4 + (t + 1))
                for f in range(KT):
                    a = A(kv[:, f, :], bc[:, t % 2, (f // 2) * DK:(f // 2 + 1) * DK], scale=wv[t % 2][:, f:f + 1])
                a.then_inc(s_kv, 1)
                split(n.plus(2))
                apart()
                ready(n)
                A(both(so[:, i * 4 + t, :]), out2(n), ACT.Sigmoid).then_inc(evac[n.c % 2], 1)

            with act.Fori(0, 2) as i:
                for t in range(4):
                    o_step(i, t)
            act.wait_ge(s_p, 1)
            A(hah[:, :, SEQ:TOK], so[:, :, SEQ:TOK]).then_inc(s_hah, 1)

            with act.Fori(0, NC) as c:
                for t in range(4):
                    n = At(S_BY + t, c, 4)
                    act.wait_ge(s_rd, c * 4 + (t + 1))
                    A(hn[t % 2][:, :], trp[t % 2][:, 0:2, :].rearrange("p a b -> p (a b)"), scale=nd[:, t % 2, 2:3])\
                        .then_inc(tre[t % 2], 1)
                    split(n.plus(2))
                    if t % 2 == 0:
                        ready(n)
                        if t == 0:
                            act.wait_ge(s_hal, 1)
                        A(both(ftmp[t // 2][:, :]), out2(n), ACT.Sigmoid).then_inc(evac[n.c % 2], 1)
                    apart()
                    act.wait_ge(s_p, c * 4 + (t + 2))
                    A(hah[:, 2 * t:2 * t + 2, bass.ds(c * P, P)], so[:, 2 * t:2 * t + 2, bass.ds(c * P, P)])\
                        .then_inc(s_hah, 1)

            with act.Fori(0, KT) as i:
                n = At(S_AY, i, 2)
                split(n.plus(2))
                A(both(ftmp[0][:, :]), out2(n), ACT.Sigmoid).then_inc(evac[n.c % 2], 1)
                split(n.plus(3))
                apart()
                act.wait_ge(s_ms, i + 1)
                A(mh[:, i, :], merged[:, i, :]).then_inc(s_mh, 1)

            with act.Fori(0, KT // 2) as i:
                for t in range(2):
                    n = At(S_WO + t, i, 2)
                    split(n.plus(2))
                    apart()
                    act.wait_ge(s_x1, i * 2 + (t + 1))
                    A(x2h[:, i * 2 + t, :], x1[:, i * 2 + t, :], scale=gains[:, 2, bass.ds(i * 2 + t, 1)]).then_inc(s_x2h, 1)

            def up_step(i, first=False, last=False):
                for t in range(2):
                    width = (DN_CUTS[t + 1] - DN_CUTS[t]) * P if last else KT * P
                    n = At(S_UP + t, i, 2)
                    if first and t == 0:
                        act.wait_ge(s_ss2, 1)
                        A(both(rbc2[:, :]), aux[:, :, 0:HALF], ACT.Sqrt, bias=eps[:, :], scale=1.0 / D_MODEL)\
                            .then_inc(s_std2, 1)
                    split(n.plus(2), width)
                    apart()
                    act.wait_ge(s_up, i * 2 + (t + 1))
                    f = i * 2 + t
                    A(conv[t][:, 0:SEQ], up[t][:, 2:2 + SEQ], ACT.Identity, scale=cwb[:, f, 2:3], bias=cwb[:, f, 3:4])\
                        .then_inc(s_tap, 1)
                    if t == 0:
                        act.wait_ge(s_cv, i * 2 + 1)
                        A(silu[:, :], conv[0][:, :], ACT.Silu).then_inc(s_sil, 1)
                apart()
                act.wait_ge(s_pr, i + 1)
                A(acth[:, i, :], silu[:, :]).then_inc(s_ah, 1)

            up_step(0, True)
            with act.Fori(1, FT - 1) as i:
                up_step(i)
            up_step(FT - 1, last=True)

            def dn_tile(i, t):
                for s in range(3):
                    n = At(S_DN + 3 * t + s, i, 6)
                    w = (3 * t + s + 2) % 3
                    split(n.plus(2), (DN_CUTS[w + 1] - DN_CUTS[w]) * P)
                dn_result(i, t)

            def dn_result(i, t):
                j = i * 2 + t
                apart()
                act.wait_ge(s_x2f, j + 1)
                A(xg[:, j, :], x1[:, j, :], scale=gains[:, 3, bass.ds(j, 1)])
                apart()
                act.wait_ge(s_accf, j + 1)
                A(sqa[:, :], x1[:, j, :], ACT.Square).then_inc(s_sqf, 1)

            with act.Fori(0, KT // 2 - 1) as i:
                for t in range(2):
                    dn_tile(i, t)
            dn_tile(3, 0)
            split(At(N_SLOTS - 1), (DN_CUTS[3] - DN_CUTS[2]) * P)
            dn_result(3, 1)
            act.wait_ge(s_ssf, 1)
            A(both(ftmp[0][:, :]), aux[:, :, 0:HALF], ACT.Sqrt, bias=eps[:, :], scale=1.0 / D_MODEL).then_inc(s_stdf, 1)

        @block.vector
        def _(dve):
            TT, TS, STT = dve.tensor_tensor, dve.tensor_scalar, dve.scalar_tensor_tensor

            def low(n, width=KT * P):
                p = n.c % 2
                dve.wait_ge(w_hi, n(1))
                TT(wlo[p][:, 0:width], raw[p][:, 0:width], whi[p][:, 0:width].bitcast(F32), ALU.subtract)\
                    .then_inc(w_lo, 1)

            def ready(n):
                dve.wait_ge(done, n(2))

            def both(t):
                return t.rearrange("p (a b) -> p a b", a=2)

            def out2(n):
                return out_ps[n.c % 2][:, :, 0:HALF]

            dve.memset(eps[:, :], EPS)
            dve.memset(mrun[:, :], 0.0).then_inc(s_init, 1)
            dve.memset(ones[:, :], 1.0).then_inc(evac[0], 1)
            dve.memset(nd[:, :, :], 0.0).then_inc(evac[1], 1)
            dve.memset(srt[:, :, :], 0.0).then_inc(tre[0], 1)
            dve.memset(dm[:, :, :, :], 0.0).then_inc(tre[1], 1)
            dve.memset(state[:, :, :], 0.0).then_inc(s_st, 1)
            low(At(0))
            dve.wait_ge(s_std, 1)
            dve.reciprocal(ftmp[0][:, :], ftmp[0][:, :])
            low(At(1))
            dve.wait_ge(s_const, 32)
            dve.drain()
            for k in range(KT + 1):
                if k < KT:
                    TT(x0[:, k, :], x0[:, k, :], ftmp[0][:, :], ALU.mult).then_inc(s_xr, 1)
                if k >= 1:
                    dve.wait_ge(s_xh, k)
                    STT(xl[:, k - 1, :], x0[:, k - 1, :], gains[:, 0, k - 1:k], xh[:, k - 1, :].bitcast(F32),
                        ALU.mult, ALU.subtract).then_inc(s_xn, 1)

            def gate_cumsums():
                evacuated(dve, At(S_GATE))
                TS(ig[:, :], ig[:, :], gb[:, 0:1], None, ALU.add)
                dve.wait_ge(s_ln, 1)
                TS(lf[:, :], fg[:, :], gb[:, 1:2], 0.0, ALU.add, ALU.min)
                dve.drain()
                TT(lf[:, :], lf[:, :], lfe[:, :], ALU.subtract)
                dve.drain()
                for c in range(NC):
                    s = slice(c * P, (c + 1) * P)
                    dve.tensor_tensor_scan(bcum[:, s], ones[0:NH, :], lf[:, s], 0.0, ALU.mult, ALU.add)

            def gate_maxima():
                dve.wait_ge(s_mp, 1)
                dve.drain()
                TT(g3[0:NH, :], ig[:, 0:SEQ], bcum[:, :], ALU.subtract)
                for c in range(NC):
                    s, e = slice(c * P, (c + 1) * P), (c + 1) * P
                    dve.drain()
                    dve.tensor_tensor_scan(mmax[:, s], g3[0:NH, s], g3[0:NH, s], mrun[:, c:c + 1], ALU.max, ALU.max)
                    dve.drain()
                    TT(mrun[:, c + 1:c + 2], bcum[:, e - 1:e], mmax[:, e - 1:e], ALU.add)
                    TS(g3[32:32 + NH, s], g3[0:NH, s], mmax[:, e - 1:e], None, ALU.subtract)

            def gate_outputs():
                dve.wait_ge(s_tri, 2)
                dve.drain()
                STT(g3[64:64 + NH, :], bcum[:, :], -1.0, mmax[:, :], ALU.mult, ALU.subtract)
                TS(ni4[:, :], ident[0:NH, 0:NH], -1.0, None, ALU.mult)
                last = mmax[:, :].rearrange("h (c t) -> h c t", c=NC)[:, :, P - 1]
                dve.drain()
                TT(bcum[:, 0:NC], mrun[:, 0:NC], last, ALU.subtract)
                TT(nmx[:, :, :], mmax[:, :].unsqueeze(1).broadcast_to([NH, NH, SEQ]),
                   ni4[:, :].unsqueeze(2).broadcast_to([NH, NH, SEQ]), ALU.mult)
                dve.drain()
                i4 = ident[0:NH, 0:NH].unsqueeze(1).broadcast_to([NH, NC, NH])
                TT(dm[:, 0, :, :], bcum[:, 0:NC].unsqueeze(2).broadcast_to([NH, NC, NH]), i4, ALU.mult)
                TT(dm[:, 1, :, :], mrun[:, 0:NC].unsqueeze(2).broadcast_to([NH, NC, NH]), i4, ALU.mult)\
                    .then_inc(s_grow, 1)

            def vb_side(jt, t):
                dve.wait_ge(tr_done, jt(1))
                dve.tensor_copy(g_tok[:, :, bass.ds(jt() * P, P)] if jt.i is not None else g_tok[:, :, jt.c * P:(jt.c + 1) * P],
                                trp[t][:, :, :]).then_inc(tre[t], 1)

            def vb_step(j):
                n = At(S_VB + j)
                if j >= 1:
                    vb_side(At(j - 1), (j - 1) % 2)
                if 1 <= j <= 3:
                    (gate_cumsums, gate_maxima, gate_outputs)[j - 1]()
                low(n.plus(2))

            low(At(S_GATE + 2))
            for j in range(8):
                vb_step(j)
            vb_side(At(7), 1)
            evacuated(dve, At(S_VB + 7))
            TT(ssq[:, :, :], gvs[:, :, :], gvs[:, :, :], ALU.mult)
            dve.drain()
            dve.tensor_reduce(cq[:, 0, :], ssq[:, :, :].rearrange("p f b -> p b f"), AX_X, ALU.add).then_inc(s_ssm, 1)
            low(At(S_Q + 2))
            low(At(S_Q + 3))
            dve.wait_ge(s_vss, 1)
            dve.tensor_reduce(rv[:, 0:NC], acct[:, :, :], AX_X, ALU.add)
            dve.wait_ge(s_ssk, 8)
            dve.tensor_copy(rv[:, NC:NC + NB], aux[:, 1, 80:88]).then_inc(s_vsr, 1)
            dve.wait_ge(s_rv, 1)
            dve.reciprocal(rv[:, :], rv[:, :])
            low(At(S_Q + 4))
            low(At(S_Q + 5))
            dve.wait_ge(s_cp, 48)
            dve.drain()

            def v_stage(j, t):
                if isinstance(j, int):
                    cols = slice(j * P, (j + 1) * P)
                else:
                    cols = bass.ds(j * P, P)
                for c in range(NC):
                    o = STT(vst[t][:, c, :], g_tok[:, c, cols], rv[:, c:c + 1], gvrow[:, cols], ALU.mult, ALU.mult)
                o.then_inc(s_vst, 1)

            def u_step(i, t, first=False):
                n = At(S_U + t, i, 2)
                j = i * 2 + t
                v_stage(j, t)
                low(n.plus(2))
                b = At(B_SP + t, i, 2)
                dve.wait_ge(tr_done, b(1))
                TT(trp[t][:, :, :], trp[t][:, :, :],
                   bs[:, i, :].unsqueeze(1).broadcast_to([P, NC, P]), ALU.add)
                dve.drain()
                evacuated(dve, n)
                TT(ftmp[t][:, 0:SEQ], ftmp[t][:, 0:SEQ], trp[t][:, :, :].rearrange("p c t -> p (c t)"), ALU.mult)\
                    .then_inc(s_hbp, 1)
                dve.wait_ge(s_hbh, i * 2 + (t + 1))
                TT(hbl[:, j, 0:SEQ], ftmp[t][:, 0:SEQ], hbh[:, j, 0:SEQ].bitcast(F32), ALU.subtract).then_inc(s_hbl, 1)
                dve.nop().then_inc(tre[t], 1)

            for t in range(2):
                u_step(0, t, True)
            with dve.Fori(1, 4) as i:
                for t in range(2):
                    u_step(i, t)
            evacuated(dve, At(S_U + 7))
            TT(ssq[:, :, :], gvs[:, :, :], rv[:, NC:NC + NB].unsqueeze(1).broadcast_to([P, KT, NB]), ALU.mult)
            dve.drain()
            TT(gvs[:, :, :], ssq[:, :, :], gains[:, 1, :].unsqueeze(2).broadcast_to([P, KT, NB]), ALU.mult)
            dve.drain()
            g4 = lambda a: a.rearrange("p (g a) b -> p g (a b)", g=NG)
            TT(g4(mixs[:, :, :]), g4(gvs[:, :, :]), w00[:, :].unsqueeze(2).broadcast_to([P, NG, 2 * NB]), ALU.mult)
            dve.drain()
            TT(g4(mixs[:, :, :]), g4(mixs[:, :, :]), bs[:, :, 0:1].broadcast_to([P, NG, 2 * NB]), ALU.add)
            dve.drain()
            TT(us[:, :, :], us[:, :, :], mixs[:, :, :], ALU.mult).then_inc(s_hbp, 1)
            dve.wait_ge(s_hbh, 9)
            TT(hbl[:, :, SEQ:TOK], us[:, :, :], hbh[:, :, SEQ:TOK].bitcast(F32), ALU.subtract).then_inc(s_hbl, 1)

            def k_side(h):
                dve.wait_ge(tr_done, B_K + h + 1)
                if h == 0:
                    dve.wait_ge(s_gcol, 1)
                for c in range(NC):
                    s = slice(c * P, (c + 1) * P)
                    o = STT(d_arg[:, s], aux[:, 1, s], gcol[:, c, h:h + 1], maskmin[:, :], ALU.add, ALU.min)
                o.then_inc(s_darg, 1)
                dve.wait_ge(s_de, h + 1)
                TT(sd[:, h, :, :].rearrange("p c t -> p (c t)"), aux[:, 0, :], d_exp[:, :], ALU.mult)
                dve.wait_ge(s_wq, h + 1)
                TT(qT[:, h, 0:SEQ], qT[:, h, 0:SEQ], wq[:, :], ALU.mult).then_inc(s_auxu, 1)

            for h in range(NH):
                if h >= 1:
                    k_side(h - 1)
                low(At(S_K + h + 2))
            k_side(NH - 1)
            with dve.Fori(0, 4) as i:
                for t in range(2):
                    low(At(S_V + t + 2, i, 2))

            R = lambda r: srt[:, r, :]
            dve.wait_ge(s_ss, 32)
            TT(R(9), R(1), R(2), ALU.add)
            dve.drain()
            TT(R(3), R(9), R(0), ALU.max)
            dve.drain()
            TT(R(4), R(9), R(3), ALU.subtract)
            TT(R(5), R(0), R(3), ALU.subtract)
            TS(R(6), R(3), -1.0, None, ALU.mult).then_inc(s_sg, 1)
            dve.wait_ge(s_srow, 1)
            h4 = lambda a: a.rearrange("p (h k) -> p h k", h=NH)
            kr, qr = srows[:, 0:512], srows[:, 512:1024]
            TT(n_t[:, :], n_s[:, :], qr, ALU.mult)
            dve.drain()
            dve.tensor_reduce(R(7), h4(n_t[:, :]), AX_X, ALU.add)
            dve.drain()
            TT(n_t[:, :], kr, qr, ALU.mult)
            dve.drain()
            dve.tensor_reduce(R(8), h4(n_t[:, :]), AX_X, ALU.add)
            dve.wait_ge(s_sge, 1)
            dve.drain()
            TT(R(8), R(8), R(5), ALU.mult)
            TT(R(7), R(7), R(4), ALU.mult)
            dve.drain()
            TT(R(9), R(8), R(7), ALU.add)
            dve.drain()
            TS(R(10), R(9), -1.0, None, ALU.mult)
            dve.drain()
            TT(R(10), R(10), R(9), ALU.max)
            dve.drain()
            TT(R(10), R(10), R(6), ALU.max)
            dve.drain()
            dve.reciprocal(R(11), R(10))
            TT(h4(n_s[:, :]), h4(n_s[:, :]), R(4).unsqueeze(2).broadcast_to([NB, NH, DK]), ALU.mult)
            TT(h4(n_t[:, :]), h4(kr), R(5).unsqueeze(2).broadcast_to([NB, NH, DK]), ALU.mult)
            dve.drain()
            TT(n_s[:, :], n_s[:, :], n_t[:, :], ALU.add)
            dve.tensor_copy(srows[:, 1024:1032].rearrange("p (c h) -> p c h", c=2), srt[:, 4:6, :])
            TT(srows[:, 1032:1036], R(4), R(11), ALU.mult)
            TT(srows[:, 1036:1040], R(8), R(11), ALU.mult).then_inc(s_srd, 1)

            def o_step(i, t):
                row, cm, b = bc[:, t % 2, :], c_ring[:, t, :, :], i * 4 + t
                pair = lambda a: a.unsqueeze(2).broadcast_to([P, NH, 2])
                fh = lambda a: a.rearrange("p (h a) -> p h a", h=NH)
                dve.wait_ge(s_bc[t % 2], i * 32 + (t // 2 + 1) * 16)
                TT(fh(wv[t % 2][:, :]), fh(vs[:, b, :]), pair(row[:, 1028:1032]), ALU.mult).then_inc(s_wv, 1)
                dve.wait_ge(s_cl[t], i * 16 + 16)
                dve.wait_ge(s_tq, i * 4 + (t + 1))
                TT(fh(cq[:, 1, :]), fh(vs[:, b, :]), pair(row[:, 1036:1040]), ALU.mult)
                dve.drain()
                dve.tensor_reduce(cq[:, 0, :], tq[t % 2][:, :, :], AX_X, ALU.add)
                dve.drain()
                TT(fh(cq[:, 2, :]), fh(cq[:, 0, :]), pair(row[:, 1032:1036]), ALU.mult)
                dve.drain()
                TT(hs[:, :, b], cq[:, 2, :], cq[:, 1, :], ALU.add)
                dve.drain()
                dve.wait_ge(s_kv, i * 4 + (t + 1))
                for f in range(KT):
                    o = STT(cm[:, f, :], cm[:, f, :], row[:, 1024 + f // 2:1025 + f // 2], kv[:, f, :], ALU.mult, ALU.add)
                o.then_inc(s_cn, 1)
                low(At(S_O + t + 2, i, 4))

            with dve.Fori(0, 2) as i:
                for t in range(4):
                    o_step(i, t)
            evacuated(dve, At(S_O + 7))
            evacuated(dve, At(S_O + 6))
            dve.drain()
            TT(so[:, :, SEQ:TOK], so[:, :, SEQ:TOK], hs[:, :, :], ALU.mult).then_inc(s_p, 1)
            dve.wait_ge(s_hah, 1)
            TT(hal[:, :, SEQ:TOK], so[:, :, SEQ:TOK], hah[:, :, SEQ:TOK].bitcast(F32), ALU.subtract).then_inc(s_hal, 1)

            for t in range(4):
                dve.wait_ge(s_cs[t], 32)
            with dve.Fori(0, NC) as c:
                for t in range(4):
                    n = At(S_BY + t, c, 4)
                    num, b = trp[t % 2][:, 2, 0:1], t % 2
                    dve.wait_ge(s_num, c * 4 + (t + 1))
                    TS(nd[:, b, 0:1], num, -1.0, None, ALU.mult)
                    dve.drain()
                    STT(nd[:, b, 1:2], num, nd[:, b, 0:1], enm[:, c, t:t + 1], ALU.max, ALU.max)
                    dve.drain()
                    dve.reciprocal(nd[:, b, 2:3], nd[:, b, 1:2]).then_inc(s_rd, 1)
                    dve.wait_ge(s_unit, c * 4 + (t + 1))
                    STT(state[:, t, :], state[:, t, :], decay[:, c, t:t + 1], aux[:, 0, 0:DVA], ALU.mult, ALU.add)\
                        .then_inc(s_st, 1)
                    low(n.plus(2))
                    dve.wait_ge(s_ht, c * 4 + (t + 1))
                    part = (slice(None), slice(2 * t, 2 * t + 2), bass.ds(c * P, P))
                    TT(so[part], so[part], aux[:, 1, 0:DV].rearrange("p (a b) -> p a b", a=2), ALU.mult).then_inc(s_p, 1)
                    if t % 2 == 1:
                        ready(n)
                        evacuated(dve, n.plus(-1))
                        TT(both(merged[:, c * 2 + t // 2, :]), both(ftmp[t // 2][:, :]), out2(n), ALU.mult)\
                            .then_inc(evac[n.c % 2], 1)
                    dve.wait_ge(s_hah, c * 4 + (t + 2))
                    TT(hal[part], so[part], hah[part].bitcast(F32), ALU.subtract).then_inc(s_hal, 1)

            with dve.Fori(0, KT) as i:
                n = At(S_AY + 1, i, 2)
                low(n.plus(1))
                ready(n)
                evacuated(dve, n.plus(-1))
                TT(both(ftmp[0][:, :]), both(ftmp[0][:, :]), out2(n), ALU.mult).then_inc(evac[n.c % 2], 1)
                low(n.plus(2))
                dve.drain()
                TT(merged[:, i, :], merged[:, i, :], ftmp[0][:, :], ALU.add).then_inc(s_ms, 1)
                dve.wait_ge(s_mh, i + 1)
                TT(ml[:, i, :], merged[:, i, :], mh[:, i, :].bitcast(F32), ALU.subtract).then_inc(s_m, 1)

            dve.wait_ge(s_xres, 16)
            with dve.Fori(0, KT // 2) as i:
                for t in range(2):
                    n = At(S_WO + t, i, 2)
                    j = i * 2 + t
                    ready(n)
                    TT(both(x1[:, j, :]), out2(n), both(xres[:, j, :]), ALU.add).then_inc(evac[n.c % 2], 1)
                    dve.drain()
                    dve.nop().then_inc(s_x1, 1)
                    low(n.plus(2))
                    dve.wait_ge(s_x2h, i * 2 + (t + 1))
                    STT(x2l[:, j, :], x1[:, j, :], gains[:, 2, bass.ds(j, 1)], x2h[:, j, :].bitcast(F32),
                        ALU.mult, ALU.subtract).then_inc(s_x2, 1)

            def hidden_low(i):
                dve.wait_ge(s_ah, i + 1)
                TT(actl[:, i, :], silu[:, :], acth[:, i, :].bitcast(F32), ALU.subtract).then_inc(s_al, 1)

            def up_step(i, first=False, last=False):
                for t in range(2):
                    n = At(S_UP + t, i, 2)
                    f = i * 2 + t
                    if first and t == 0:
                        dve.memset(up[0][:, 0:2], 0.0)
                        dve.memset(up[1][:, 0:2], 0.0)
                        dve.wait_ge(s_std2, 1)
                        dve.reciprocal(rbc2[:, :], rbc2[:, :])
                        dve.drain()
                    ready(n)
                    if not first:
                        dve.wait_ge(s_nc, i * 2 + (t - 1))
                    TT(both(up[t][:, 2:2 + TOK]), out2(n), both(rbc2[:, :]), ALU.mult).then_inc(evac[n.c % 2], 1)
                    dve.drain()
                    dve.nop().then_inc(s_up, 1)
                    if t == 0 and not first:
                        hidden_low(i - 1)
                    low(n.plus(2), (DN_CUTS[t + 1] - DN_CUTS[t]) * P if last else KT * P)
                    STT(conv[t][:, SEQ:TOK], up[t][:, 2 + SEQ:2 + TOK], cwb[:, f, 2:3], sconv[:, f, :], ALU.mult, ALU.add)
                    dve.wait_ge(s_tap, i * 2 + (t + 1))
                    STT(conv[t][:, 0:SEQ], up[t][:, 1:1 + SEQ], cwb[:, f, 1:2], conv[t][:, 0:SEQ], ALU.mult, ALU.add)
                    dve.drain()
                    STT(conv[t][:, 0:SEQ], up[t][:, 0:SEQ], cwb[:, f, 0:1], conv[t][:, 0:SEQ], ALU.mult, ALU.add)\
                        .then_inc(s_cv, 1)
                dve.drain()
                dve.wait_ge(s_sil, i + 1)
                TT(silu[:, :], silu[:, :], conv[1][:, :], ALU.mult).then_inc(s_pr, 1)

            dve.wait_ge(s_scv, 1)
            up_step(0, True)
            with dve.Fori(1, FT - 1) as i:
                up_step(i)
            up_step(FT - 1, last=True)
            hidden_low(FT - 1)

            def dn_tile(i, t, final=False):
                for s in range(1 if final else 3):
                    w = (3 * t + s + 2) % 3
                    low(At(S_DN + 3 * t + s + 2, i, 6), (DN_CUTS[w + 1] - DN_CUTS[w]) * P)
                j = i * 2 + t
                dve.wait_ge(done, At(S_DN + 3 * t + 2, i, 6)(2))
                bank = (S_DN + t) % 2
                o = out_ps[bank][:, :, 0:HALF]
                TT(both(x1[:, j, :]), o, both(x1[:, j, :]), ALU.add).then_inc(evac[bank], 1)
                dve.drain()
                dve.nop().then_inc(s_x2f, 1)
                dve.wait_ge(s_sqf, j + 1)
                TT(acc[:, :], acc[:, :], sqa[:, :], ALU.add).then_inc(s_accf, 1)
                dve.drain()

            dve.memset(acc[:, :], 0.0).then_inc(s_accf, 1)
            with dve.Fori(0, KT // 2 - 1) as i:
                for t in range(2):
                    dn_tile(i, t)
            dn_tile(3, 0)
            dn_tile(3, 1, True)
            dve.wait_ge(s_stdf, 1)
            dve.reciprocal(ftmp[0][:, :], ftmp[0][:, :]).then_inc(s_rf, 1)
            dve.drain()
            for j in range(5):
                TT(y[:, j, :], xg[:, j, :], ftmp[0][:, :], ALU.mult).then_inc(s_y, 1)

        @block.gpsimd
        def _(pool):
            pool.dma_start(ws[:, :, :], ins["w_sT"]).then_inc(s_ws, 16)
            pool.dma_start(gvrow[:, :], ins["g_vrow"].broadcast_to([P, D_MODEL])).then_inc(s_cp, 16)
            pool.dma_start(bs[:, :, :].rearrange("p g t -> p (g t)"), ins["b_s"].broadcast_to([P, NG * P])).then_inc(s_cp, 16)
            pool.dma_start(w00[:, :], ins["w_s00"].broadcast_to([P, NG])).then_inc(s_cp, 16)
            pool.memset(ident[:, :], 0.0)
            pool.memset(maskmin[:, :], 0.0)
            pool.drain()
            pool.affine_select(out=ident[:, :], in_=ident[:, :], compare_op=ALU.not_equal, fill=1.0, base=0,
                               pattern=[[-1, P]], channel_multiplier=1)
            pool.affine_select(out=maskmin[:, :], in_=maskmin[:, :], compare_op=ALU.is_ge, fill=BIG, base=0,
                               pattern=[[1, P]], channel_multiplier=-1).then_inc(s_tri, 1)
            pool.wait_ge(s_ws, 16)
            pool.affine_select(out=ws[:, :, :], in_=ws[:, :, :], compare_op=ALU.is_ge, fill=0.0, base=0,
                               pattern=[[0, NG], [1, P]], channel_multiplier=-1).then_inc(s_tri, 1)
            pool.wait_ge(s_xn, KT)
            pool.memset(g3[:, :], 0.0)
            pool.memset(v_tok[:, :, :, DV:DVA], 1.0)
            pool.memset(acct[:, :, :], 0.0).then_inc(s_mp, 1)
            pool.drain()

            def squares(jt, t):
                pool.wait_ge(tre[t], jt.half(2))
                g = g_tok[:, :, bass.ds(jt() * P, P)]
                pool.tensor_tensor(sqt[:, :, :], g, g, ALU.mult)
                pool.drain()
                o = pool.tensor_tensor(acct[:, :, :], acct[:, :, :], sqt[:, :, :], ALU.add)
                pool.drain()
                return o

            with pool.Fori(0, 3) as i:
                for t in range(2):
                    squares(At(B_VB + t, i, 2), t)
            pool.wait_ge(tre[0], 5)
            pool.tensor_tensor(sqt[:, :, :], g_tok[:, :, 6 * P:7 * P], g_tok[:, :, 6 * P:7 * P], ALU.mult)
            pool.drain()
            pool.tensor_tensor(acct[:, :, :], acct[:, :, :], sqt[:, :, :], ALU.add)
            pool.wait_ge(tre[1], 5)
            pool.drain()
            pool.tensor_tensor(sqt[:, :, :], g_tok[:, :, 7 * P:8 * P], g_tok[:, :, 7 * P:8 * P], ALU.mult)
            pool.drain()
            pool.tensor_tensor(acct[:, :, :], acct[:, :, :], sqt[:, :, :], ALU.add).then_inc(s_vss, 1)
            pool.wait_ge(s_hbl, 9)
            pool.dma_start(n_s[:, :], ins["n_state"]).then_inc(s_ss, 16)
            pool.dma_start(srt[:, 2, :], ins["m_state"]).then_inc(s_ss, 16)
            pool.dma_start(outs["v_sample"], gvs[:, :, :]).then_inc(s_out, 16)
            pool.wait_ge(s_auxu, NH)
            for b in range(4):
                pool.dma_start(c_ring[:, b, :, :], ins["C_state"][b]).then_inc(s_cl[b], 16)
            pool.dma_start(outs["m_prompt"], mrun[:, NC:NC + 1]).then_inc(s_out, 16)
            pool.wait_ge(s_srd, 1)
            pool.dma_start(scratch, srows[:, :]).then_inc(s_scr, 16)
            pool.dma_start(outs["n_sample"], n_s[:, :]).then_inc(s_nst, 16)
            pool.dma_start(outs["m_sample"], srt[:, 3, :]).then_inc(s_out, 16)
            pool.wait_ge(s_nst, 16)
            pool.wait_ge(s_scr, 16)
            for b in range(2):
                pool.dma_start(bc[:, b, :], scratch[b:b + 1, :].broadcast_to([P, ROW])).then_inc(s_bc[b], 16)

            def c_times_q(b):
                t = b % 4
                pool.wait_ge(s_bc[b % 2], (b // 2 + 1) * 16)
                pool.wait_ge(s_cl[t], (b // 4 + 1) * 16)
                if b >= 2:
                    pool.wait_ge(s_cn, b - 1)
                pair = lambda a: a.rearrange("p (h a) k -> p h a k", h=NH)
                pool.tensor_tensor(pair(tq[b % 2][:, :, :]), pair(c_ring[:, t, :, :]),
                                   bc[:, b % 2, 512:1024].rearrange("p (h k) -> p h k", h=NH).unsqueeze(2)
                                   .broadcast_to([P, NH, 2, DK]), ALU.mult).then_inc(s_tq, 1)

            def c_turn(i, t, load_row=True, load_c=True):
                b = i * 4 + t
                if b + 1 < NB:
                    c_times_q(b + 1)
                pool.wait_ge(s_cn, b + 1)
                pool.dma_start(outs["C_sample"][b], c_ring[:, t, :, :]).then_inc(s_cs[t], 16)
                if load_row:
                    nb = bass.ds(b + 2, 1) if not isinstance(b, int) else slice(b + 2, b + 3)
                    pool.dma_start(bc[:, t % 2, :], scratch[nb, :].broadcast_to([P, ROW])).then_inc(s_bc[t % 2], 16)
                if load_c:
                    pool.wait_ge(s_cs[t], 16)
                    pool.dma_start(c_ring[:, t, :, :], ins["C_state"][b + 4]).then_inc(s_cl[t], 16)

            c_times_q(0)
            for t in range(4):
                c_turn(0, t)
            for t in range(4):
                c_turn(1, t, load_row=t < 2, load_c=False)

            def stage_unit(c, t, first=False):
                if not (first and t < 2):
                    pool.wait_ge(s_unit, c * 4 + (t - 1))
                span = bass.ds(c * P, P) if not isinstance(c, int) else slice(c * P, (c + 1) * P)
                pool.tensor_copy(sds[t % 2][:, :], sd[:, t, c, :])
                pool.tensor_copy(qs[t % 2][:, :], qT[:, t, span])
                pool.tensor_tensor(kw[t % 2][:, :], k_tok[:, c, t, :], wlast[:, c, t:t + 1].broadcast_to([P, P]), ALU.mult)\
                    .then_inc(s_stg, 1)

            for t in range(4):
                stage_unit(0, t, True)
            with pool.Fori(1, NC) as c:
                for t in range(4):
                    stage_unit(c, t)

            pool.wait_ge(s_unit, NC * NH)
            pool.dma_start(xres[:, :, :], ins["x_all"]).then_inc(s_xres, 16)
            pool.wait_ge(s_st, NC * NH + 1)
            pool.dma_start(outs["state"], state[:, :, :]).then_inc(s_out, 16)
            pool.wait_ge(done, S_WO + 1)
            pool.dma_start(cst[:, :, :, :], ins["conv_state"]).then_inc(s_ffl, 16)
            pool.dma_start(cwb[:, :, :], ins["conv_wb"]).then_inc(s_ffl, 16)
            pool.wait_ge(s_ffl, 32)
            pool.dma_start(outs["conv_old"], cst[:, :, 1, :]).then_inc(s_out, 16)
            wb = lambda k: cwb[:, :, k:k + 1].broadcast_to([P, 2 * FT, NB])
            pool.tensor_tensor(sconv[:, :, :], cst[:, :, 0, :], wb(0), ALU.mult)
            pool.tensor_tensor(sct[:, :, :], cst[:, :, 1, :], wb(1), ALU.mult)
            pool.drain()
            pool.tensor_tensor(sconv[:, :, :], sconv[:, :, :], wb(3), ALU.add)
            pool.drain()
            pool.tensor_tensor(sconv[:, :, :], sconv[:, :, :], sct[:, :, :], ALU.add).then_inc(s_scv, 1)
            pool.memset(acc[:, :], 0.0)
            pool.drain()
            for j in range(KT):
                pool.wait_ge(s_x1, j + 1)
                pool.tensor_tensor(sqa[:, :], x1[:, j, :], x1[:, j, :], ALU.mult)
                pool.drain()
                o = pool.tensor_tensor(acc[:, :], acc[:, :], sqa[:, :], ALU.add)
                pool.drain()
            pool.nop().then_inc(s_acc, 1)

            with pool.Fori(0, FT) as i:
                for t in range(2):
                    pool.wait_ge(s_up, i * 2 + (t + 1))
                    pool.tensor_copy(nconv[:, i * 2 + t, :], up[t][:, SEQ:2 + TOK]).then_inc(s_nc, 1)
            pool.wait_ge(s_nc, 2 * FT)
            pool.dma_start(outs["conv_new"], nconv[:, :, :]).then_inc(s_out, 16)
            pool.wait_ge(s_rf, 1)
            for j in range(5, KT):
                pool.tensor_tensor(y[:, j, :], xg[:, j, :], ftmp[0][:, :], ALU.mult).then_inc(s_yp, 1)
            for t in range(4):
                pool.wait_ge(s_cs[t], 32)
            pool.wait_ge(s_out, 16 * 6)

        @block.tensor
        def _(pe):
            def MM(*a, **k):
                return pe.matmul(*a, **k)

            def tile(n, hi, lo, k0=0, nk=KT, bank=None, use=None, start=True, stop=True, mid=None, mid_at=3, each=None, end=None):
                p = n.c % 2
                pe.wait_ge(w_lo, n(1))
                if start:
                    pe.wait_ge(evac[p if bank is None else bank], n.half(1) if use is None else use)
                o = out_ps[p if bank is None else bank]
                for k in range(nk):
                    if each is not None:
                        pe.wait_ge(each, k + 1)
                    w = slice(k * P, (k + 1) * P)
                    for wt, x in ((whi[p], hi), (whi[p], lo), (wlo[p], hi)):
                        for a in range(2):
                            m = MM(o[:, a, 0:HALF], wt[:, w], x[:, k0 + k, a * HALF:(a + 1) * HALF],
                                   start=start and k == 0 and wt is whi[p] and x is hi,
                                   stop=stop and k == nk - 1 and wt is wlo[p])
                    if k == mid_at and mid is not None:
                        mid()
                m.then_inc(done, 1)
                if end is not None:
                    end()

            def transposes(b, evn):
                evacuated(pe, evn)
                pe.wait_ge(tre[b.c % 2], b.half(1))
                for c in range(NC):
                    m = pe.transpose(trp[b.c % 2][:, c, :], ftmp[b.c % 2][:, c * P:(c + 1) * P], ident[:, :])
                m.then_inc(tr_done, 1)

            pe.wait_ge(evac[0], 1)
            for k in range(KT):
                pe.wait_ge(s_sq, k + 1)
                for a in range(2):
                    m = MM(aux[:, a, 0:HALF], ones[:, :], sq[k % 2][:, a * HALF:(a + 1) * HALF],
                           start=k == 0, stop=k == KT - 1)
                m.then_inc(s_ssk if k < KT - 1 else done, 1)
            pe.wait_ge(s_tri, 2)

            def vb_tile(i, t, first=False):
                n = At(S_VB + t, i, 2)
                b = At(B_VB + t - 1, i, 2) if not (first and t == 0) else None
                tile(n, xh, xl, mid=(lambda: transposes(b, n.plus(-1))) if b is not None else None)

            tile(At(S_GATE), xh, xl, each=s_xn)
            for t in range(2):
                vb_tile(0, t, True)
            with pe.Fori(1, 4) as i:
                for t in range(2):
                    vb_tile(i, t)

            def v_sums():
                pe.wait_ge(s_ssm, 1)
                MM(aux[:, 1, 80:88], ones[:, :], cq[:, 0, :], start=True, stop=True).then_inc(s_ssk, 1)

            tile(At(S_Q), xh, xl, mid=lambda: transposes(At(B_VB + 7), At(S_VB + 7)))
            tile(At(S_Q + 1), xh, xl, mid=v_sums)
            for j in range(2, NH):
                tile(At(S_Q + j), xh, xl)

            def spatial(i, t):
                b = At(B_SP + t, i, 2)
                pe.wait_ge(s_vst, i * 2 + (t + 1))
                pe.wait_ge(tre[t], b.half(1))
                for c in range(NC):
                    m = MM(trp[t][:, c, :], vst[t][:, c, :], ws[:, i, :], start=True, stop=True)
                m.then_inc(tr_done, 1)

            def gate_columns():
                pe.wait_ge(s_grow, 1)
                for c in range(NC):
                    pe.transpose(aux[:, 0, c * P:(c + 1) * P], g3[:, c * P:(c + 1) * P], ident[:, :])
                MM(aux[:, 1, 0:32], ones[0:NH, :], dm[:, :, :, :].rearrange("k a c h -> k (a c h)"), start=True, stop=True)
                MM(aux[0:NB, 1, 64:68], ig[:, SEQ:TOK], ident[0:NH, 0:NH], start=True, stop=True)
                MM(aux[0:NB, 1, 68:72], lf[:, SEQ:TOK], ident[0:NH, 0:NH], start=True, stop=True).then_inc(s_gcd, 1)

            for t in range(2):
                tile(At(S_U + t), xh, xl, end=lambda: spatial(0, t))
            with pe.Fori(1, 4) as i:
                for t in range(2):
                    tile(At(S_U + t, i, 2), xh, xl, end=lambda: spatial(i, t))
            gate_columns()
            def k_side(h):
                evacuated(pe, At(S_K + h))
                if h == 0:
                    pe.wait_ge(s_gcol, 1)
                else:
                    pe.wait_ge(s_auxu, h)
                for c in range(NC):
                    s = slice(c * P, (c + 1) * P)
                    MM(aux[:, 0, s], ftmp[h % 2][:, s], qT[:, h, s], start=True, stop=True)
                MM(aux[:, 1, :], ones[0:NH, :], nmx[:, h, :], start=True, stop=True)
                transposes(At(B_K + h), At(S_K + h))

            for h in range(NH):
                tile(At(S_K + h), xh, xl, mid=(lambda: k_side(h - 1)) if h >= 1 else None)

            def sample_rows():
                pe.wait_ge(s_auxu, NH)
                for h in range(NH):
                    pe.transpose(aux[0:NB, 0, h * P:(h + 1) * P], ks[:, h, :], ident[:, :])
                    m = pe.transpose(aux[0:NB, 1, h * P:(h + 1) * P], qT[:, h, SEQ:TOK], ident[:, :])
                m.then_inc(s_rowd, 1)

            tile(At(S_V), xh, xl, mid=lambda: k_side(NH - 1))
            tile(At(S_V + 1), xh, xl, mid=lambda: transposes(At(B_V), At(S_V)), end=sample_rows)
            with pe.Fori(1, 4) as i:
                for t in range(2):
                    tile(At(S_V + t, i, 2), xh, xl,
                         mid=lambda: transposes(At(B_V + t - 1, i, 2), At(S_V + t - 1, i, 2)))
            transposes(At(B_V + 7), At(S_V + 7))

            with pe.Fori(0, 4) as i:
                for t in range(2):
                    tile(At(S_O + t, i, 2), xh, xl)

            def unit_products(c, t):
                b = At(B_UNIT + t, c, 4)
                pe.wait_ge(s_stg, c * 4 + (t + 1))
                pe.wait_ge(tre[t % 2], b.half(1))
                pe.wait_ge(s_st, c * 4 + (t + 1))
                num = trp[t % 2][:, :, :].rearrange("p a b -> p (a b)")[:, 0:DVA]
                MM(num, qs[t % 2][:, :], state[:, t, :], start=True, stop=False)
                MM(num, sds[t % 2][:, :], v_tok[:, c, t, :], start=False, stop=True).then_inc(s_num, 1)
                MM(aux[:, 0, 0:DVA], kw[t % 2][:, :], v_tok[:, c, t, :], start=True, stop=True).then_inc(s_unit, 1)

            def unit_transposes(c, t):
                b = At(B_UNIT + t, c, 4)
                pe.wait_ge(tre[t % 2], b.half(2))
                for a in range(2):
                    m = pe.transpose(aux[:, 1, a * P:(a + 1) * P], hn[t % 2][:, a * P:(a + 1) * P], ident[:, :])
                m.then_inc(s_ht, 1)

            pe.wait_ge(s_hbl, 9)
            with pe.Fori(0, NC) as c:
                for t in range(4):
                    xs = (xh, xl) if t % 2 == 0 else (hbh, hbl)
                    tile(At(S_BY + t, c, 4), *xs, mid_at=1, mid=lambda: unit_products(c, t), end=lambda: unit_transposes(c, t))

            with pe.Fori(0, KT) as i:
                tile(At(S_AY, i, 2), xh, xl)
                pe.wait_ge(s_hal, NC * NH + 1)
                tile(At(S_AY + 1, i, 2), hah, hal)

            tile(At(S_WO), mh, ml, each=s_m)
            tile(At(S_WO + 1), mh, ml)
            with pe.Fori(1, 4) as i:
                for t in range(2):
                    tile(At(S_WO + t, i, 2), mh, ml)

            def norm_sums(ready, count, signal):
                pe.wait_ge(ready, count)
                for a in range(2):
                    m = MM(aux[:, a, 0:HALF], ones[:, :], acc[:, a * HALF:(a + 1) * HALF], start=True, stop=True)
                m.then_inc(signal, 1)

            tile(At(S_UP), x2h, x2l, each=s_x2, end=lambda: norm_sums(s_acc, 1, s_ss2))
            tile(At(S_UP + 1), x2h, x2l)
            with pe.Fori(1, FT) as i:
                for t in range(2):
                    tile(At(S_UP + t, i, 2), x2h, x2l)

            def dn_pair(i, first=False):
                for s in range(6):
                    t, q = s // 3, s % 3
                    bank = (S_DN + t) % 2
                    n = At(S_DN + s, i, 6)
                    if first and s < 3:
                        pe.wait_ge(s_al, FT - 1 if q < 2 else FT)
                    tile(n, acth, actl, k0=DN_CUTS[q], nk=DN_CUTS[q + 1] - DN_CUTS[q], bank=bank,
                         use=At(S_DN + t, i, 2).half(1), start=q == 0, stop=q == 2)

            dn_pair(0, True)
            with pe.Fori(1, KT // 2) as i:
                dn_pair(i)
            norm_sums(s_accf, KT + 1, s_ssf)


_OUTS = {
    "y": (P, KT, TOK), "state": (P, NH, DVA), "m_prompt": (NH, 1), "conv_new": (P, 2 * FT, 2 + NB),
    "conv_old": (P, 2 * FT, NB), "C_sample": (NB, P, KT, DK), "n_sample": (NB, NH * DK), "m_sample": (NB, NH),
    "v_sample": (P, KT, NB),
}


def kernel(**inputs):
    import numpy as np
    import concourse.bacc as bacc
    from concourse.bass_utils import run_bass_kernel_spmd as run

    a = {k: np.asarray(v) for k, v in inputs.items()}
    w_in = a["w_in"][0]

    def slot(w, c):
        return w[:, c:c + P].reshape(KT, P, P).transpose(1, 0, 2).reshape(P, KT * P)

    hk, hv = NH * DK, NH * DV
    q0, k0, v0, o0 = 0, hk, 2 * hk, 2 * hk + hv
    i0 = o0 + hv
    f0, u0 = i0 + NH, i0 + 2 * NH
    vb0, ga0, gb0 = u0 + D_MODEL, u0 + 2 * D_MODEL, u0 + 3 * D_MODEL
    gates = slot(np.concatenate([w_in[:, i0:i0 + 32], w_in[:, f0:f0 + 96]], axis=1), 0)
    slots = [gates]
    for c0, m in ((vb0, 8), (q0, 4), (u0, 8), (k0, 4), (v0, 8), (o0, 8)):
        slots += [slot(w_in, c0 + j * P) for j in range(m)]
    for j in range(8):
        slots += [slot(w_in, gb0 + j * P), slot(a["w_branch_b"][0], j * P)]
    for j in range(8):
        slots += [slot(w_in, ga0 + j * P), slot(a["w_branch_a"][0], j * P)]
    slots += [slot(a["w_out"][0], j * P) for j in range(8)]
    for j in range(FT):
        slots += [slot(a["w_up"][0], j * P), slot(a["w_up"][0], D_FF + j * P)]
    w_dn = a["w_down"][0].reshape(FT, P, KT, P).transpose(2, 1, 0, 3).reshape(KT, P, FT * P)

    x_all = np.concatenate([a["x_prompt"][0], a["x_sample"][:, 0]], axis=0).T.reshape(KT, P, TOK)
    cols = lambda v: v.reshape(KT, P).T
    order = [f for j in range(FT) for f in (j, FT + j)]
    ff = lambda v: v.reshape(v.shape[:-1] + (2 * FT, P))[..., order, :]
    conv_wb = np.concatenate([ff(a["conv_w"][0]), ff(a["conv_b"])], axis=0).transpose(2, 1, 0)
    arrays = {
        "w_slots": np.stack(slots), "w_dn": w_dn, "xT": x_all, "x_all": x_all.transpose(1, 0, 2),
        "gains": np.stack([cols(a["g_norm1"][0]), cols(a["g_vnorm"][0]), cols(a["g_norm2"][0]), cols(a["g_final"])], axis=1),
        "gate_b": np.stack([a["b_igate"][0], a["b_fgate"][0]], axis=1),
        "g_vrow": a["g_vnorm"], "b_s": a["b_spatial"].reshape(1, NG * P),
        "w_sT": a["w_spatial"][0].transpose(2, 0, 1), "w_s00": a["w_spatial"][:, :, 0, 0],
        "C_state": a["state_mlstm_C"][0].reshape(NB, NH, 2, P, DK).transpose(0, 3, 1, 2, 4).reshape(NB, P, KT, DK),
        "n_state": a["state_mlstm_n"][0].reshape(NB, NH * DK), "m_state": a["state_mlstm_m"][0],
        "conv_state": ff(a["state_ffn_conv"][0]).transpose(3, 2, 1, 0), "conv_wb": conv_wb,
    }
    nc = bacc.Bacc("TRN2", target_bir_lowering=False, num_devices=1)
    feed, ins, outs = {}, {}, {}
    for name, v in arrays.items():
        v = np.ascontiguousarray(v)
        feed[f"in_{name}"] = v
        ins[name] = nc.dram_tensor(f"in_{name}", v.shape, mybir.dt.from_np(v.dtype), kind="ExternalInput").ap()
    for name, shape in _OUTS.items():
        outs[name] = nc.dram_tensor(f"out_{name}", shape, F32, kind="ExternalOutput").ap()
    hybrid_layer(nc, ins, outs)
    r = run(nc, [feed], core_ids=[0]).results[0]
    r = {name: np.asarray(r[f"out_{name}"]) for name in _OUTS}

    tok = r["y"].transpose(2, 1, 0).reshape(TOK, D_MODEL)
    back = np.argsort(order)
    rows = lambda v: v.transpose(2, 1, 0)[:, back, :].reshape(-1, 2 * D_FF)
    new = rows(r["conv_new"])
    return (
        tok[None, :SEQ], tok[SEQ:, None],
        r["state"][:, :, 0:DV].transpose(1, 2, 0)[None, None], r["state"][:, :, DV].T[None, None],
        r["m_prompt"].reshape(1, 1, NH), new[None, None, 0:2],
        r["C_sample"].reshape(NB, P, NH, 2, DK).transpose(0, 2, 3, 1, 4).reshape(1, NB, NH, DV, DK),
        r["n_sample"].reshape(1, NB, NH, DK), r["m_sample"][None],
        np.stack([rows(r["conv_old"]), new[2:]], axis=1)[None],
        r["v_sample"].transpose(2, 1, 0).reshape(1, NB, 1, D_MODEL),
    )
```

```python
from contextlib import ExitStack

import concourse.bass as bass
from concourse import mybir

F32 = mybir.dt.float32
F32R = mybir.dt.float32r
ALU = mybir.AluOpType
ACT = mybir.ActivationFunctionType
AX_X = mybir.AxisListType.X

P = 128
D_MODEL, SEQ, NB = 1024, 512, 8
NH, DK, DV = 4, 128, 256
NG, D_FF, CONV_W = 4, 2816, 3
EPS = 1e-6
TOK = SEQ + NB
HALF = TOK // 2
KT = D_MODEL // P
NC = SEQ // P
FT = D_FF // P
DVA = DV + 1
BIG = -3.0e38

S_GATE = 0
S_VB = S_GATE + 1
S_Q = S_VB + 8
S_U = S_Q + NH
S_K = S_U + 8
S_V = S_K + NH
S_O = S_V + 8
S_BY = S_O + 8
S_AY = S_BY + 16
S_WO = S_AY + 16
S_UP = S_WO + 8
S_DN = S_UP + 2 * FT
DN_CUTS = (0, 8, 15, 22)
N_SLOTS = S_DN + 3 * KT
Y_DVE = 5

B_VB, B_SP, B_K, B_V, B_UNIT = 0, 8, 16, 20, 28
ROWB = 2 * NH * DK
ROW = ROWB + 4 * NH


class At:

    def __init__(self, c, i=None, s=0):
        self.c, self.i, self.s = c, i, s

    def __call__(self, extra=0):
        return self.c + extra if self.i is None else self.i * self.s + (self.c + extra)

    def half(self, extra=0):
        return self.c // 2 + extra if self.i is None else self.i * (self.s // 2) + (self.c // 2 + extra)

    def plus(self, k):
        return At(self.c + k, self.i, self.s)


def hybrid_layer(nc, ins, outs):
    with ExitStack() as ctx:
        base = nc.sbuf_base + 64 - nc.sbuf_base % 64
        ARENA = 190528
        fence = ctx.enter_context(nc.sbuf_tensor("arena", [P, (ARENA + 64) // 4], F32))
        assert fence is not None

        def at(name, shape, offset, dt=F32):
            return nc.alloc_sbuf_tensor_at(name, shape, dt, offset=base + offset)

        def sb(name, shape, dt=F32):
            return ctx.enter_context(nc.sbuf_tensor(name, shape, dt))

        def sem(name):
            return ctx.enter_context(nc.semaphore(name))

        XB = KT * TOK * 4
        xh = at("xh", [P, KT, TOK], 0, F32R)
        xl = at("xl", [P, KT, TOK], XB, F32R)
        x2h = at("x2h", [P, KT, TOK], 0, F32R)
        x2l = at("x2l", [P, KT, TOK], XB, F32R)
        xg = at("xg", [P, KT, TOK], 0)
        y = at("y", [P, KT, TOK], XB)
        xuh = at("xuh", [P, KT, TOK], 2 * XB, F32R)
        xul = at("xul", [P, KT, TOK], 3 * XB, F32R)
        rbc1 = at("rbc1", [P, TOK], 5 * XB + 12288)
        hbh = at("hbh", [P, KT, TOK], 2 * XB, F32R)
        hbl = at("hbl", [P, KT, TOK], 3 * XB, F32R)
        mh = at("mh", [P, KT, TOK], 2 * XB, F32R)
        ml = at("ml", [P, KT, TOK], 3 * XB, F32R)
        actl = at("actl", [P, FT, TOK], 2 * XB, F32R)
        g_tok = at("g_tok", [P, NC, D_MODEL], 4 * XB)
        gvrow = at("gvrow", [P, D_MODEL], 5 * XB)
        nmx = at("nmx", [NH, NH, SEQ], 5 * XB + 4096)
        d_arg = at("d_arg", [P, SEQ], 5 * XB + 12288)
        d_exp = at("d_exp", [P, SEQ], 5 * XB + 14336)
        srows = at("srows", [NB, ROW], 4 * XB + 8320)
        tq = [at(f"tq{t}", [P, KT, DK], 4 * XB + 8320 + 4160 * t) for t in range(2)]
        n_s = at("n_s", [NB, NH * DK], 4 * XB + 12480)
        n_t = at("n_t", [NB, NH * DK], 4 * XB + 14528)
        hah = at("hah", [P, KT, TOK], 4 * XB, F32R)
        hal = at("hal", [P, KT, TOK], 5 * XB, F32R)
        so = at("so", [P, KT, TOK], 5 * XB)
        F0 = 79040
        cst = at("cst", [P, 2 * FT, 2, NB], F0)
        cwb = at("cwb", [P, 2 * FT, 4], F0 + 2816)
        sconv = at("sconv", [P, 2 * FT, NB], F0 + 3520)
        nconv = at("nconv", [P, 2 * FT, 2 + NB], F0 + 4928)
        up = [at(f"up{t}", [P, 2 + TOK], F0 + 6688 + 2112 * t) for t in range(2)]
        conv = [at(f"conv{t}", [P, TOK], F0 + 10912 + 2080 * t) for t in range(2)]
        silu = at("silu", [P, TOK], F0 + 15072)
        rbc2 = at("rbc2", [P, TOK], F0 + 17152)
        sct = at("sct", [P, 2 * FT, NB], F0 + 6688)
        assert F0 + 19232 <= 6 * XB
        M0 = 6 * XB
        x0 = at("x0", [P, KT, TOK], M0)
        c_ring = at("c_ring", [P, 4, KT, DK], M0)
        merged = at("merged", [P, KT, TOK], M0)
        x1 = at("x1", [P, KT, TOK], M0)
        Q0 = 7 * XB
        qT = at("qT", [P, NH, TOK], Q0)
        k_tok = at("k_tok", [P, NC, NH, DK], Q0 + 8320)
        v_tok = at("v_tok", [P, NC, NH, DVA], Q0 + 16512)
        sd = at("sd", [P, NH, NC, P], Q0 + 32960)
        G0 = Q0 + 16512
        ig = at("ig", [NH, TOK], G0)
        fg = at("fg", [NH, TOK], G0 + 2080)
        lf = at("lf", [NH, TOK], G0 + 4160)
        bcum = at("bcum", [NH, SEQ], G0 + 6240)
        mmax = at("mmax", [NH, SEQ], G0 + 8288)
        g3 = at("g3", [P, SEQ], G0 + 10336)
        lfe = at("lfe", [NH, TOK], G0 + 12384)
        assert Q0 + 41152 <= 165952
        xres = at("xres", [P, KT, TOK], Q0)
        acth = at("acth", [P, FT, TOK], Q0, F32R)
        R0 = 165952
        raw = [at(f"raw{t}", [P, KT * P], R0 + 4096 * t) for t in range(2)]
        whi = [at(f"whi{t}", [P, KT * P], R0 + 8192 + 4096 * t, F32R) for t in range(2)]
        wlo = [at(f"wlo{t}", [P, KT * P], R0 + 16384 + 4096 * t, F32R) for t in range(2)]
        assert R0 + 24576 == ARENA
        ident = sb("ident", [P, P])
        ones = sb("ones", [P, P])
        maskmin = sb("maskmin", [P, P])
        sp_at = nc.sbuf_base + 64 - nc.sbuf_base % 64
        sp_place = sb("sp_place", [P, 4160 // 4])
        assert sp_place is not None
        row2 = nc.alloc_sbuf_tensor_at("row2", [P, ROWB], F32, offset=sp_at)
        ws = nc.alloc_sbuf_tensor_at("ws", [P, NG, P], F32, offset=sp_at)
        bs = nc.alloc_sbuf_tensor_at("bs", [P, NG, P], F32, offset=sp_at + 2048)
        state = sb("state", [P, NH, DVA])
        ftmp_at = nc.sbuf_base + 64 - nc.sbuf_base % 64
        ftmp_place = sb("ftmp_place", [P, 2 * TOK + 16])
        assert ftmp_place is not None
        ftmp = [nc.alloc_sbuf_tensor_at(f"ftmp{t}", [P, TOK], F32, offset=ftmp_at + 2080 * t) for t in range(2)]
        rbcf = ftmp[0]
        rows = [at("row0", [P, ROWB], 4 * XB), at("row1", [P, ROWB], 4 * XB + 4160), row2,
                nc.alloc_sbuf_tensor_at("row3", [P, ROWB], F32, offset=ftmp_at)]
        stage_at = nc.sbuf_base + 64 - nc.sbuf_base % 64
        stage = sb("stage", [P, 5184 // 4])
        assert stage is not None

        def st(name, shape, offset):
            return nc.alloc_sbuf_tensor_at(name, shape, F32, offset=stage_at + offset)

        sq = [st(f"sq{t}", [P, TOK], 2080 * t) for t in range(2)]
        acct = st("acct", [P, NC, P], 0)
        sqt = st("sqt", [P, NC, P], 2048)
        vst = [st(f"vst{t}", [P, NC, P], 2048 * t) for t in range(2)]
        wq = st("wq", [P, SEQ], 0)
        kv = st("kv", [P, KT, DK], 0)
        hn = [st(f"hn{t}", [P, DV], 1024 * t) for t in range(2)]
        sc = st("sc", [P, NB, 4 * NH], 4096)
        wv = st("wv", [P, NB, KT], 4608)
        wvq = st("wvq", [P, NB, KT], 4864)

        def spare(name, offset):
            return nc.alloc_sbuf_tensor_at(name, [P, P], F32, offset=sp_at + offset)

        sds = [spare(f"sds{t}", 512 * t) for t in range(2)]
        qs = [spare(f"qs{t}", 1024 + 512 * t) for t in range(2)]
        kw = [spare(f"kw{t}", 2048 + 512 * t) for t in range(2)]
        acc = st("acc", [P, TOK], 0)
        sqa = st("sqa", [P, TOK], 2080)

        gains = sb("gains", [P, 4, KT])
        w00 = sb("w00", [P, NG])
        gb = sb("gb", [NH, 2])
        eps = sb("eps", [P, 1])
        unused = sb("unused", [P, 1])
        mrun = sb("mrun", [NH, NC + 1])
        ni4 = sb("ni4", [NH, NH])
        dm = sb("dm", [NH, 2, NC, NH])
        gcol = sb("gcol", [P, NC, NH])
        wlast = sb("wlast", [P, NC, NH])
        enm = sb("enm", [P, NC, NH])
        decay = sb("decay", [P, NC, NH])
        mpb = sb("mpb", [P, NC, NH])
        rv = sb("rv", [P, NC + NB])
        gvs = sb("gvs", [P, KT, NB])
        ssq = sb("ssq", [P, KT, NB])
        mixs = sb("mixs", [P, KT, NB])
        us = sb("us", [P, KT, NB])
        ks = sb("ks", [P, NH, NB])
        vs = sb("vs", [P, NB, KT])
        hs = sb("hs", [P, NB, KT])
        cq = sb("cq", [P, KT])
        srt = sb("srt", [NB, 12, NH])
        nd = sb("nd", [P, 2, 3])

        out_ps = [ctx.enter_context(nc.psum_tensor(f"out{t}", [P, 2, 512], F32)) for t in range(2)]
        trp = [ctx.enter_context(nc.psum_tensor(f"trp{t}", [P, NC, P], F32)) for t in range(2)]
        aux = ctx.enter_context(nc.psum_tensor("aux", [P, 2, 512], F32))
        scratch = nc.dram_tensor("scratch", (NB, ROW), F32).ap()

        s_x = [sem(f"x_loaded{k}") for k in range(KT // 2)]
        s_g = sem("gains_loaded")
        s_const = sem("consts_loaded")
        s_cp = sem("spatial_consts_loaded")
        s_ws = sem("spatial_weights_loaded")
        s_ss = sem("sample_states_loaded")
        s_init = sem("consts_made")
        s_tri = sem("triangles_made")
        s_sq = [sem("even_square_ready"), sem("odd_square_ready")]
        s_xuh = sem("x_gain_hi")
        s_xu = sem("x_gain_lo")
        s_r1 = sem("x_scale_ready")
        s_raw = sem("vb_scaled")
        s_ssk = sem("square_summed")
        s_std = sem("std_ready")
        s_xr = sem("x_scaled")
        s_xh = sem("x_hi")
        s_xn = sem("x_lo")
        w_loaded = [sem(f"w_loaded{t}") for t in range(2)]
        w_hi = sem("w_hi")
        w_lo = sem("w_lo")
        done = sem("slots_done")
        evac = [sem(f"bank_emptied{t}") for t in range(2)]
        tr_done = sem("transposed")
        tre = [sem(f"tr_emptied{t}") for t in range(2)]
        s_vss = sem("v_squares_summed")
        s_vsr = sem("v_square_sums_ready")
        s_rv = sem("v_norm_std")
        s_ssm = sem("v_sample_sums")
        s_vst = sem("v_staged")
        s_hbp = sem("hb_product")
        s_hbh = sem("hb_hi")
        s_hbl = sem("hb_lo")
        s_ln = sem("softplus_ready")
        s_grow = sem("gate_rows")
        s_gcd = sem("gate_columns_done")
        s_gcol = sem("gate_columns")
        s_darg = sem("decay_exponents")
        s_wq = sem("inter_weights")
        s_de = sem("decay_matrix")
        s_auxu = sem("scores_used")
        s_rowd = sem("sample_rows_done")
        s_srow = sem("sample_rows")
        s_sg = sem("sample_gates")
        s_sge = sem("sample_gate_exps")
        s_srd = sem("sample_row_complete")
        s_scr = sem("scratch_written")
        s_bc = [sem(f"row_loaded{t}") for t in range(4)]
        s_scal = sem("sample_scalars_loaded")
        s_cl = [sem(f"C_loaded{t}") for t in range(4)]
        s_cs = [sem(f"C_stored{t}") for t in range(4)]
        s_nst = sem("n_sample_stored")
        s_tq = sem("C_times_q")
        s_kv = sem("kv_products")
        s_cn = sem("C_updated")
        s_stg = sem("unit_staged")
        s_num = sem("unit_numerator")
        s_unit = sem("unit_products_done")
        s_st = sem("state_ready")
        s_rd = sem("unit_denominator")
        s_ht = sem("unit_transposed")
        s_p = sem("ha_product")
        s_hah = sem("ha_hi")
        s_hal = sem("ha_lo")
        s_ms = sem("merged_sum")
        s_mh = sem("merged_hi")
        s_m = sem("merged_lo")
        s_xres = sem("residual_loaded")
        s_x1 = sem("x1_ready")
        s_x2h = sem("x2_hi")
        s_x2 = sem("x2_lo")
        s_acc = sem("norm2_sums")
        s_ss2 = sem("norm2_broadcast")
        s_std2 = sem("norm2_std")
        s_ffl = sem("ffn_consts_loaded")
        s_scv = sem("sample_conv_ready")
        s_up = sem("up_scaled")
        s_tap = sem("tap2_ready")
        s_cv = sem("conv_ready")
        s_sil = sem("silu_ready")
        s_pr = sem("hidden_product")
        s_ah = sem("hidden_hi")
        s_al = sem("hidden_lo")
        s_nc = sem("conv_rows_kept")
        s_x2f = sem("result_ready")
        s_sqf = sem("result_squared")
        s_xg = sem("results_gained")
        s_accf = sem("final_sums")
        s_ssf = sem("final_broadcast")
        s_stdf = sem("final_std")
        s_rf = sem("final_scale")
        s_y = sem("y_dve")
        s_yp = sem("y_pool")
        s_out = sem("outputs_stored")
        s_yout = sem("y_stored")
        s_mp = sem("memory_prepared")

        def evacuated(eng, n):
            eng.wait_ge(evac[n.c % 2], n.half(2))

        block = ctx.enter_context(nc.Block())

        @block.sync
        def _(sp):
            def load(n, src, width=KT * P):
                p = n.c % 2
                if n.c >= 2:
                    sp.wait_ge(w_lo, n(-1))
                sp.dma_start(raw[p][:, 0:width], src).then_inc(w_loaded[p], 16)

            def load_slots(first, last):
                with sp.Fori(0, (last - first) // 2) as i:
                    for t in range(2):
                        n = At(first + t, i, 2)
                        load(n, wp[n()])
                if (last - first) % 2:
                    load(At(last - 1), wp[last - 1])

            wp = ins["w_slots"]
            for k in (0, 1, 3):
                sp.dma_start(x0[:, 2 * k:2 * k + 2, :], ins["x_all"][:, 2 * k:2 * k + 2, :]).then_inc(s_x[k], 16)
            for n in range(2):
                load(At(n), wp[n])
            load_slots(2, S_K)
            sp.wait_ge(s_xn, KT)
            for b in range(4):
                sp.dma_start(c_ring[:, b, :, :], ins["C_state"][b]).then_inc(s_cl[b], 16)
                load(At(S_K + b), wp[S_K + b])
            load_slots(S_V, S_O)
            sp.wait_ge(s_scr, 16)
            sp.dma_start(sc[:, :, :], scratch[:, ROWB:ROW].unsqueeze(0).broadcast_to([P, NB, 4 * NH])).then_inc(s_scal, 16)

            def load_row(b):
                sp.dma_start(rows[b % 4][:, :], scratch[b:b + 1, 0:ROWB].broadcast_to([P, ROWB])).then_inc(s_bc[b % 4], 16)

            for b in range(3):
                load_row(b)
                load(At(S_O + b), wp[S_O + b])
            sp.wait_ge(tr_done, B_UNIT)
            load_row(3)
            load(At(S_O + 3), wp[S_O + 3])
            for b in range(NB):
                t = b % 4
                sp.wait_ge(s_cn, b + 2)
                sp.dma_start(outs["C_sample"][b], c_ring[:, t, :, :]).then_inc(s_cs[t], 16)
                load(At(S_O + 4 + b), wp[S_O + 4 + b])
                if b + 4 < NB:
                    load_row(b + 4)
                    sp.wait_ge(s_cs[t], 16)
                    sp.dma_start(c_ring[:, t, :, :], ins["C_state"][b + 4]).then_inc(s_cl[t], 16)
            load_slots(S_O + 4 + NB, S_DN)
            with sp.Fori(0, KT // 2) as i:
                for s in range(6):
                    a, b = DN_CUTS[s % 3], DN_CUTS[s % 3 + 1]
                    load(At(S_DN + s, i, 6), ins["w_dn"][i * 2 + s // 3, :, a * P:b * P], (b - a) * P)
            for a in range(2):
                h = slice(a * HALF, (a + 1) * HALF)
                for ready_, count, j0, j1 in ((s_y, 2, 0, 2), (s_y, Y_DVE, 2, Y_DVE), (s_yp, KT - Y_DVE, Y_DVE, KT)):
                    sp.wait_ge(ready_, a * (Y_DVE if ready_ is s_y else KT - Y_DVE) + count)
                    sp.dma_start(outs["y"][:, j0:j1, h], y[:, j0:j1, h]).then_inc(s_yout, 16)
            sp.wait_ge(s_yout, 16 * 6)

        @block.scalar
        def _(act):
            def A(out, in_, func=ACT.Copy, **kw_):
                return act.activation(out, in_, func, **kw_)

            def split(n, width=KT * P):
                p = n.c % 2
                act.wait_ge(w_loaded[p], n.half(1) * 16)
                if n.c >= 2:
                    act.wait_ge(done, n())
                A(whi[p][:, 0:width], raw[p][:, 0:width]).then_inc(w_hi, 1)

            def ready(n):
                act.wait_ge(done, n(2))

            def apart():
                act.wait_ge(done, 1)

            def both(t):
                return t.rearrange("p (a b) -> p a b", a=2)

            def out2(n):
                return out_ps[n.c % 2][:, :, 0:HALF]

            def smp(n):
                return out_ps[n.c % 2][:, 1, HALF - NB:HALF]

            def table_of_sqrt():
                A(unused[:, :], eps[:, :], ACT.Sqrt)

            act.dma_start(gains[:, :, :], ins["gains"]).then_inc(s_g, 16)
            act.dma_start(x0[:, 4:6, :], ins["x_all"][:, 4:6, :]).then_inc(s_x[2], 16)
            act.dma_start(gb[:, :], ins["gate_b"]).then_inc(s_const, 16)
            act.wait_ge(s_init, 1)
            table_of_sqrt()
            act.wait_ge(s_g, 16)
            for k in range(KT):
                act.wait_ge(s_x[k // 2], 16)
                if k % 2 == 0:
                    if k >= 2:
                        act.wait_ge(s_ssk, k - 1)
                    A(sq[0][:, :], x0[:, k, :], ACT.Square).then_inc(s_sq[0], 1)
                if k == KT - 2:
                    split(At(0))
                A(xuh[:, k, :], x0[:, k, :], scale=gains[:, 0, k:k + 1]).then_inc(s_xuh, 1)
            split(At(1))
            act.wait_ge(done, 1)
            act.wait_ge(s_init, 1)
            A(both(rbc1[:, :]), aux[:, :, 0:HALF], ACT.Sqrt, bias=eps[:, :], scale=1.0 / D_MODEL).then_inc(s_std, 1)

            def normed_hi(k):
                act.wait_ge(s_xr, k + 1)
                A(xh[:, k, :], x0[:, k, :], scale=gains[:, 0, k:k + 1]).then_inc(s_xh, 1)

            def scaled_vb(j):
                act.wait_ge(s_raw, j + 1)
                A(gvs[:, j, :], ftmp[j][:, SEQ:TOK], ACT.Gelu_apprx_tanh)
                act.drain()
                A(ftmp[j][:, :], ftmp[j][:, :], ACT.Gelu_apprx_tanh).then_inc(evac[(S_VB + j) % 2], 1)

            split(At(2))
            for k in range(4):
                normed_hi(k)
            split(At(3))
            for k in range(4, 6):
                normed_hi(k)
            scaled_vb(0)
            for k in range(6, KT):
                normed_hi(k)
            split(At(4))
            scaled_vb(1)

            def vb_step(i, t):
                n = At(S_VB + t, i, 2)
                split(n.plus(2))
                apart()
                ready(n)
                act.wait_ge(tr_done, n(-2))
                A(gvs[:, i * 2 + t, :], smp(n), ACT.Gelu_apprx_tanh)
                A(both(ftmp[t][:, :]), out2(n), ACT.Gelu_apprx_tanh).then_inc(evac[n.c % 2], 1)

            vb_step(1, 0)
            evacuated(act, At(S_GATE))
            act.wait_ge(s_const, 16)
            A(lfe[:, :], fg[:, :], ACT.Abs, bias=gb[:, 1:2])
            act.drain()
            A(lfe[:, :], lfe[:, :], ACT.Exp, scale=-1.0)
            vb_step(1, 1)
            act.drain()
            A(lfe[:, :], lfe[:, :], ACT.Ln, bias=ones[0:NH, 0:1]).then_inc(s_ln, 1)
            with act.Fori(2, 4) as i:
                for t in range(2):
                    vb_step(i, t)

            def q_step(j):
                n = At(S_Q + j)
                if j == 2:
                    act.wait_ge(s_vsr, 1)
                    A(rv[:, :], rv[:, :], ACT.Sqrt, bias=eps[:, :], scale=1.0 / D_MODEL).then_inc(s_rv, 1)
                split(n.plus(2))
                ready(n)
                A(both(qT[:, j, :]), out2(n)).then_inc(evac[n.c % 2], 1)

            for j in range(NH):
                q_step(j)

            def u_step(i, t, first=False):
                n = At(S_U + t, i, 2)
                j = i * 2 + t
                split(n.plus(2))
                apart()
                ready(n)
                if first:
                    act.wait_ge(tr_done, B_VB + 7 + t)
                else:
                    act.wait_ge(s_hbl, i * 2 + (t - 1))
                A(us[:, j, :], smp(n), ACT.Gelu_apprx_tanh)
                A(both(ftmp[t][:, :]), out2(n), ACT.Gelu_apprx_tanh).then_inc(evac[n.c % 2], 1)
                apart()
                act.wait_ge(s_hbp, i * 2 + (t + 1))
                A(hbh[:, j, 0:SEQ], ftmp[t][:, 0:SEQ]).then_inc(s_hbh, 1)

            for t in range(2):
                u_step(0, t, True)
            with act.Fori(1, 4) as i:
                for t in range(2):
                    u_step(i, t)

            act.wait_ge(s_gcd, 1)
            A(gcol[:, :, :], aux[:, 0, :].rearrange("p (c t) -> p c t", c=NC)[:, :, 0:NH])
            A(wlast[:, :, :], aux[:, 0, :].rearrange("p (c t) -> p c t", c=NC)[:, :, 32:32 + NH], ACT.Exp)
            A(enm[:, :, :], aux[:, 0, :].rearrange("p (c t) -> p c t", c=NC)[:, :, 64:64 + NH], ACT.Exp)
            A(decay[:, :, :], aux[:, 1, 0:16].rearrange("p (c h) -> p c h", c=NC), ACT.Exp)
            A(mpb[:, :, :], aux[:, 1, 16:32].rearrange("p (c h) -> p c h", c=NC))
            A(srt[:, 0:2, :], aux[0:NB, 1, 64:72].rearrange("p (c h) -> p c h", c=2)).then_inc(s_gcol, 1)
            act.wait_ge(s_hbp, 9)
            A(hbh[:, :, SEQ:TOK], us[:, :, :]).then_inc(s_hbh, 1)

            def k_side(h):
                act.wait_ge(s_darg, h + 1)
                A(d_exp[:, :], d_arg[:, :], ACT.Exp).then_inc(s_de, 1)
                for c in range(NC):
                    a = A(wq[:, c * P:(c + 1) * P], aux[:, 1, c * P:(c + 1) * P], ACT.Exp, bias=mpb[:, c, h:h + 1])
                a.then_inc(s_wq, 1)
                A(k_tok[:, :, h, :], trp[h % 2][:, :, :]).then_inc(tre[h % 2], 1)

            for h in range(NH):
                n = At(S_K + h)
                if h >= 1:
                    k_side(h - 1)
                split(n.plus(2))
                ready(n)
                if h < 2:
                    act.wait_ge(s_hbl, 9)
                else:
                    act.wait_ge(tr_done, B_K + h - 1)
                A(ks[:, h, :], smp(n), scale=DK ** -0.5)
                A(both(ftmp[h % 2][:, :]), out2(n), scale=DK ** -0.5).then_inc(evac[n.c % 2], 1)

            def v_side(i, t):
                b = At(B_V + t, i, 2)
                apart()
                act.wait_ge(tr_done, b(1))
                A(v_tok[:, :, i, t * P:(t + 1) * P], trp[t][:, :, :]).then_inc(tre[t], 1)

            def v_step(i, t, first=False):
                n = At(S_V + t, i, 2)
                if first and t == 0:
                    k_side(NH - 1)
                else:
                    v_side(i - 1 + t, 1 - t)
                split(n.plus(2))
                apart()
                ready(n)
                act.wait_ge(tr_done, At(B_V + t, i, 2)(-1))
                A(vs[:, :, i * 2 + t], smp(n))
                A(both(ftmp[t][:, :]), out2(n)).then_inc(evac[n.c % 2], 1)

            for t in range(2):
                v_step(0, t, True)
            act.wait_ge(s_rowd, 1)
            A(srows[:, 0:512], aux[0:NB, 0, :])
            A(srows[:, 512:1024], aux[0:NB, 1, :]).then_inc(s_srow, 1)
            act.wait_ge(s_sg, 1)
            A(srt[:, 4:7, :], srt[:, 4:7, :], ACT.Exp).then_inc(s_sge, 1)
            with act.Fori(1, 4) as i:
                for t in range(2):
                    v_step(i, t)
            v_side(3, 1)

            def o_step(i, t):
                n = At(S_O + t, i, 4)
                b = i * 4 + t
                apart()
                act.wait_ge(s_bc[t], i * 16 + 16)
                act.wait_ge(s_cn, b + 1)
                for f in range(KT):
                    a = A(kv[:, f, :], rows[t][:, (f // 2) * DK:(f // 2 + 1) * DK], scale=wv[:, b, f:f + 1])
                a.then_inc(s_kv, 1)
                split(n.plus(2))
                apart()
                ready(n)
                A(both(so[:, b, :]), out2(n), ACT.Sigmoid).then_inc(evac[n.c % 2], 1)

            with act.Fori(0, 2) as i:
                for t in range(4):
                    o_step(i, t)
            act.wait_ge(s_p, 1)
            A(hah[:, :, SEQ:TOK], so[:, :, SEQ:TOK]).then_inc(s_hah, 1)

            with act.Fori(0, NC) as c:
                for t in range(4):
                    n = At(S_BY + t, c, 4)
                    act.wait_ge(s_rd, c * 4 + (t + 1))
                    A(hn[t % 2][:, :], trp[t % 2][:, 0:2, :].rearrange("p a b -> p (a b)"), scale=nd[:, t % 2, 2:3])\
                        .then_inc(tre[t % 2], 1)
                    split(n.plus(2))
                    if t % 2 == 0:
                        ready(n)
                        if t == 0:
                            act.wait_ge(s_hal, 1)
                        A(both(ftmp[t // 2][:, :]), out2(n), ACT.Sigmoid).then_inc(evac[n.c % 2], 1)
                    apart()
                    act.wait_ge(s_p, c * 4 + (t + 2))
                    A(hah[:, 2 * t:2 * t + 2, bass.ds(c * P, P)], so[:, 2 * t:2 * t + 2, bass.ds(c * P, P)])\
                        .then_inc(s_hah, 1)

            with act.Fori(0, KT) as i:
                n = At(S_AY, i, 2)
                split(n.plus(2))
                A(both(ftmp[0][:, :]), out2(n), ACT.Sigmoid).then_inc(evac[n.c % 2], 1)
                split(n.plus(3))
                apart()
                act.wait_ge(s_ms, i + 1)
                A(mh[:, i, :], merged[:, i, :]).then_inc(s_mh, 1)

            with act.Fori(0, KT // 2) as i:
                for t in range(2):
                    n = At(S_WO + t, i, 2)
                    split(n.plus(2))
                    apart()
                    act.wait_ge(s_x1, i * 2 + (t + 1))
                    A(x2h[:, i * 2 + t, :], x1[:, i * 2 + t, :], scale=gains[:, 2, bass.ds(i * 2 + t, 1)]).then_inc(s_x2h, 1)

            def up_step(i, first=False, last=False):
                for t in range(2):
                    width = (DN_CUTS[t + 1] - DN_CUTS[t]) * P if last else KT * P
                    n = At(S_UP + t, i, 2)
                    if first and t == 0:
                        act.wait_ge(s_ss2, 1)
                        A(both(rbc2[:, :]), aux[:, :, 0:HALF], ACT.Sqrt, bias=eps[:, :], scale=1.0 / D_MODEL)\
                            .then_inc(s_std2, 1)
                    split(n.plus(2), width)
                    apart()
                    act.wait_ge(s_up, i * 2 + (t + 1))
                    f = i * 2 + t
                    A(conv[t][:, 0:SEQ], up[t][:, 2:2 + SEQ], ACT.Identity, scale=cwb[:, f, 2:3], bias=cwb[:, f, 3:4])\
                        .then_inc(s_tap, 1)
                    if t == 0:
                        act.wait_ge(s_cv, i * 2 + 1)
                        A(silu[:, :], conv[0][:, :], ACT.Silu).then_inc(s_sil, 1)
                apart()
                act.wait_ge(s_pr, i + 1)
                A(acth[:, i, :], silu[:, :]).then_inc(s_ah, 1)

            up_step(0, True)
            with act.Fori(1, FT - 1) as i:
                up_step(i)
            up_step(FT - 1, last=True)

            def dn_tile(i, t):
                for s in range(3):
                    n = At(S_DN + 3 * t + s, i, 6)
                    w = (3 * t + s + 2) % 3
                    split(n.plus(2), (DN_CUTS[w + 1] - DN_CUTS[w]) * P)
                dn_result(i, t)

            def dn_result(i, t):
                j = i * 2 + t
                apart()
                act.wait_ge(s_x2f, j + 1)
                act.wait_ge(s_accf, j + 1)
                A(sqa[:, :], x1[:, j, :], ACT.Square).then_inc(s_sqf, 1)
                A(xg[:, j, :], x1[:, j, :], scale=gains[:, 3, bass.ds(j, 1)])

            with act.Fori(0, KT // 2 - 1) as i:
                for t in range(2):
                    dn_tile(i, t)
            dn_tile(3, 0)
            split(At(N_SLOTS - 1), (DN_CUTS[3] - DN_CUTS[2]) * P)
            table_of_sqrt()
            act.nop().then_inc(s_xg, 1)
            act.wait_ge(s_accf, KT)
            for a in range(2):
                h = slice(a * HALF, (a + 1) * HALF)
                act.wait_ge(s_x2f, KT + a)
                A(sqa[:, h], x1[:, KT - 1, h], ACT.Square).then_inc(s_sqf, 1)
            for a in range(2):
                act.wait_ge(s_ssf, a + 1)
                A(rbcf[:, a * HALF:(a + 1) * HALF], aux[:, a, 0:HALF], ACT.Sqrt, bias=eps[:, :], scale=1.0 / D_MODEL)\
                    .then_inc(s_stdf, 1)
            A(xg[:, KT - 1, :], x1[:, KT - 1, :], scale=gains[:, 3, KT - 1:KT]).then_inc(s_xg, 1)

        @block.vector
        def _(dve):
            TT, TS, STT = dve.tensor_tensor, dve.tensor_scalar, dve.scalar_tensor_tensor

            def low(n, width=KT * P):
                p = n.c % 2
                dve.wait_ge(w_hi, n(1))
                TT(wlo[p][:, 0:width], raw[p][:, 0:width], whi[p][:, 0:width].bitcast(F32), ALU.subtract)\
                    .then_inc(w_lo, 1)

            def ready(n):
                dve.wait_ge(done, n(2))

            def both(t):
                return t.rearrange("p (a b) -> p a b", a=2)

            def out2(n):
                return out_ps[n.c % 2][:, :, 0:HALF]

            dve.memset(eps[:, :], EPS)
            dve.memset(mrun[:, :], 0.0).then_inc(s_init, 1)
            dve.memset(ones[:, :], 1.0).then_inc(evac[0], 1)
            dve.memset(nd[:, :, :], 0.0).then_inc(evac[1], 1)
            dve.memset(srt[:, :, :], 0.0).then_inc(tre[0], 1)
            dve.memset(dm[:, :, :, :], 0.0).then_inc(tre[1], 1)
            dve.memset(state[:, :, :], 0.0).then_inc(s_st, 1)
            dve.wait_ge(s_g, 16)
            for r in range(KT // 2):
                dve.wait_ge(s_x[r], 16)
                if r >= 1:
                    dve.wait_ge(s_ssk, 2 * r)
                TT(sq[1][:, :], x0[:, 2 * r + 1, :], x0[:, 2 * r + 1, :], ALU.mult).then_inc(s_sq[1], 1)
                if r == KT // 2 - 1:
                    low(At(0))
                for k in (2 * r, 2 * r + 1):
                    dve.wait_ge(s_xuh, k + 1)
                    STT(xul[:, k, :], x0[:, k, :], gains[:, 0, k:k + 1], xuh[:, k, :].bitcast(F32),
                        ALU.mult, ALU.subtract).then_inc(s_xu, 1)
            low(At(1))
            dve.wait_ge(s_std, 1)
            dve.reciprocal(rbc1[:, :], rbc1[:, :]).then_inc(s_r1, 1)
            dve.drain()
            ready(At(S_GATE))
            for at0, rows_ in ((0, ig), (32, fg)):
                o = TT(both(rows_[:, :]), out_ps[0][at0:at0 + NH, :, 0:HALF], both(rbc1[at0:at0 + NH, :]), ALU.mult)
            o.then_inc(evac[0], 1)

            def normed_low(k):
                dve.wait_ge(s_xh, k + 1)
                STT(xl[:, k, :], x0[:, k, :], gains[:, 0, k:k + 1], xh[:, k, :].bitcast(F32),
                    ALU.mult, ALU.subtract).then_inc(s_xn, 1)

            def scaled_vb(j):
                ready(At(S_VB + j))
                TT(both(ftmp[j][:, :]), out2(At(S_VB + j)), both(rbc1[:, :]), ALU.mult).then_inc(s_raw, 1)

            low(At(2))
            for k in range(4):
                normed_low(k)
            scaled_vb(0)
            low(At(3))
            for k in range(4, KT):
                normed_low(k)
            scaled_vb(1)

            def gate_cumsums():
                dve.wait_ge(s_const, 16)
                TS(ig[:, :], ig[:, :], gb[:, 0:1], None, ALU.add)
                dve.wait_ge(s_ln, 1)
                TS(lf[:, :], fg[:, :], gb[:, 1:2], 0.0, ALU.add, ALU.min)
                dve.drain()
                TT(lf[:, :], lf[:, :], lfe[:, :], ALU.subtract)
                dve.drain()
                for c in range(NC):
                    s = slice(c * P, (c + 1) * P)
                    dve.tensor_tensor_scan(bcum[:, s], ones[0:NH, :], lf[:, s], 0.0, ALU.mult, ALU.add)

            def gate_maxima():
                dve.wait_ge(s_mp, 1)
                dve.drain()
                TT(g3[0:NH, :], ig[:, 0:SEQ], bcum[:, :], ALU.subtract)
                for c in range(NC):
                    s, e = slice(c * P, (c + 1) * P), (c + 1) * P
                    dve.drain()
                    dve.tensor_tensor_scan(mmax[:, s], g3[0:NH, s], g3[0:NH, s], mrun[:, c:c + 1], ALU.max, ALU.max)
                    dve.drain()
                    TT(mrun[:, c + 1:c + 2], bcum[:, e - 1:e], mmax[:, e - 1:e], ALU.add)
                    TS(g3[32:32 + NH, s], g3[0:NH, s], mmax[:, e - 1:e], None, ALU.subtract)

            def gate_outputs():
                dve.wait_ge(s_tri, 1)
                dve.drain()
                STT(g3[64:64 + NH, :], bcum[:, :], -1.0, mmax[:, :], ALU.mult, ALU.subtract)
                TS(ni4[:, :], ident[0:NH, 0:NH], -1.0, None, ALU.mult)
                last = mmax[:, :].rearrange("h (c t) -> h c t", c=NC)[:, :, P - 1]
                dve.drain()
                TT(bcum[:, 0:NC], mrun[:, 0:NC], last, ALU.subtract)
                TT(nmx[:, :, :], mmax[:, :].unsqueeze(1).broadcast_to([NH, NH, SEQ]),
                   ni4[:, :].unsqueeze(2).broadcast_to([NH, NH, SEQ]), ALU.mult)
                dve.drain()
                i4 = ident[0:NH, 0:NH].unsqueeze(1).broadcast_to([NH, NC, NH])
                TT(dm[:, 0, :, :], bcum[:, 0:NC].unsqueeze(2).broadcast_to([NH, NC, NH]), i4, ALU.mult)
                TT(dm[:, 1, :, :], mrun[:, 0:NC].unsqueeze(2).broadcast_to([NH, NC, NH]), i4, ALU.mult)\
                    .then_inc(s_grow, 1)

            def vb_side(j):
                dve.wait_ge(tr_done, B_VB + j + 1)
                dve.tensor_copy(g_tok[:, :, j * P:(j + 1) * P], trp[j % 2][:, :, :]).then_inc(tre[j % 2], 1)

            def vb_step(j):
                n = At(S_VB + j)
                vb_side(j - 1)
                if 4 <= j <= 6:
                    (gate_cumsums, gate_maxima, gate_outputs)[j - 4]()
                low(n.plus(2))

            for j in range(1, 8):
                vb_step(j)
            vb_side(7)
            evacuated(dve, At(S_VB + 7))
            TT(ssq[:, :, :], gvs[:, :, :], gvs[:, :, :], ALU.mult)
            dve.drain()
            dve.tensor_reduce(cq[:, :], ssq[:, :, :].rearrange("p f b -> p b f"), AX_X, ALU.add).then_inc(s_ssm, 1)
            low(At(S_Q + 2))
            low(At(S_Q + 3))
            dve.wait_ge(s_vss, 1)
            dve.tensor_reduce(rv[:, 0:NC], acct[:, :, :], AX_X, ALU.add)
            dve.wait_ge(s_ssk, 8)
            dve.tensor_copy(rv[:, NC:NC + NB], aux[:, 1, 80:88]).then_inc(s_vsr, 1)
            dve.wait_ge(s_rv, 1)
            dve.reciprocal(rv[:, :], rv[:, :])
            low(At(S_Q + 4))
            low(At(S_Q + 5))
            dve.wait_ge(s_cp, 48)
            dve.drain()

            def v_stage(i, t):
                cols = bass.ds(i * 2 * P + t * P, P) if not isinstance(i, int) else slice((i * 2 + t) * P, (i * 2 + t + 1) * P)
                for c in range(NC):
                    o = STT(vst[t][:, c, :], g_tok[:, c, cols], rv[:, c:c + 1], gvrow[:, cols], ALU.mult, ALU.mult)
                o.then_inc(s_vst, 1)

            def u_step(i, t, last=False):
                n = At(S_U + t, i, 2)
                j = i * 2 + t
                low(n.plus(2))
                b = At(B_SP + t, i, 2)
                dve.wait_ge(tr_done, b(1))
                TT(trp[t][:, :, :], trp[t][:, :, :],
                   bs[:, i, :].unsqueeze(1).broadcast_to([P, NC, P]), ALU.add)
                dve.drain()
                evacuated(dve, n)
                TT(ftmp[t][:, 0:SEQ], ftmp[t][:, 0:SEQ], trp[t][:, :, :].rearrange("p c t -> p (c t)"), ALU.mult)\
                    .then_inc(s_hbp, 1)
                if not last:
                    v_stage(i + t, 1 - t)
                dve.wait_ge(s_hbh, j + 1)
                TT(hbl[:, j, 0:SEQ], ftmp[t][:, 0:SEQ], hbh[:, j, 0:SEQ].bitcast(F32), ALU.subtract).then_inc(s_hbl, 1)
                dve.nop().then_inc(tre[t], 1)

            v_stage(0, 0)
            for t in range(2):
                u_step(0, t)
            with dve.Fori(1, 3) as i:
                for t in range(2):
                    u_step(i, t)
            u_step(3, 0)
            u_step(3, 1, last=True)
            evacuated(dve, At(S_U + 7))
            TT(ssq[:, :, :], gvs[:, :, :], rv[:, NC:NC + NB].unsqueeze(1).broadcast_to([P, KT, NB]), ALU.mult)
            dve.drain()
            TT(gvs[:, :, :], ssq[:, :, :], gains[:, 1, :].unsqueeze(2).broadcast_to([P, KT, NB]), ALU.mult)
            dve.drain()
            g4 = lambda a: a.rearrange("p (g a) b -> p g (a b)", g=NG)
            TT(g4(mixs[:, :, :]), g4(gvs[:, :, :]), w00[:, :].unsqueeze(2).broadcast_to([P, NG, 2 * NB]), ALU.mult)
            dve.drain()
            TT(g4(mixs[:, :, :]), g4(mixs[:, :, :]), bs[:, :, 0:1].broadcast_to([P, NG, 2 * NB]), ALU.add)
            dve.drain()
            TT(us[:, :, :], us[:, :, :], mixs[:, :, :], ALU.mult).then_inc(s_hbp, 1)
            dve.wait_ge(s_hbh, 9)
            TT(hbl[:, :, SEQ:TOK], us[:, :, :], hbh[:, :, SEQ:TOK].bitcast(F32), ALU.subtract).then_inc(s_hbl, 1)

            def k_side(h):
                dve.wait_ge(tr_done, B_K + h + 1)
                if h == 0:
                    dve.wait_ge(s_gcol, 1)
                for c in range(NC):
                    s = slice(c * P, (c + 1) * P)
                    o = STT(d_arg[:, s], aux[:, 1, s], gcol[:, c, h:h + 1], maskmin[:, :], ALU.add, ALU.min)
                o.then_inc(s_darg, 1)
                dve.wait_ge(s_de, h + 1)
                TT(sd[:, h, :, :].rearrange("p c t -> p (c t)"), aux[:, 0, :], d_exp[:, :], ALU.mult)
                dve.wait_ge(s_wq, h + 1)
                TT(qT[:, h, 0:SEQ], qT[:, h, 0:SEQ], wq[:, :], ALU.mult).then_inc(s_auxu, 1)

            for h in range(NH):
                if h >= 1:
                    k_side(h - 1)
                low(At(S_K + h + 2))
            k_side(NH - 1)
            R = lambda r: srt[:, r, :]
            dve.wait_ge(s_ss, 32)
            TT(R(9), R(1), R(2), ALU.add)
            dve.drain()
            TT(R(3), R(9), R(0), ALU.max)
            dve.drain()
            TT(R(4), R(9), R(3), ALU.subtract)
            TT(R(5), R(0), R(3), ALU.subtract)
            TS(R(6), R(3), -1.0, None, ALU.mult).then_inc(s_sg, 1)
            low(At(S_V + 2))
            low(At(S_V + 3))
            dve.wait_ge(s_srow, 1)
            h4 = lambda a: a.rearrange("p (h k) -> p h k", h=NH)
            kr, qr = srows[:, 0:512], srows[:, 512:1024]
            TT(n_t[:, :], n_s[:, :], qr, ALU.mult)
            dve.drain()
            dve.tensor_reduce(R(7), h4(n_t[:, :]), AX_X, ALU.add)
            dve.drain()
            TT(n_t[:, :], kr, qr, ALU.mult)
            dve.drain()
            dve.tensor_reduce(R(8), h4(n_t[:, :]), AX_X, ALU.add)
            low(At(S_V + 4))
            dve.wait_ge(s_sge, 1)
            dve.drain()
            TT(R(8), R(8), R(5), ALU.mult)
            TT(R(7), R(7), R(4), ALU.mult)
            dve.drain()
            TT(R(9), R(8), R(7), ALU.add)
            dve.drain()
            TS(R(10), R(9), -1.0, None, ALU.mult)
            dve.drain()
            TT(R(10), R(10), R(9), ALU.max)
            dve.drain()
            TT(R(10), R(10), R(6), ALU.max)
            dve.drain()
            dve.reciprocal(R(11), R(10))
            TT(h4(n_s[:, :]), h4(n_s[:, :]), R(4).unsqueeze(2).broadcast_to([NB, NH, DK]), ALU.mult)
            TT(h4(n_t[:, :]), h4(kr), R(5).unsqueeze(2).broadcast_to([NB, NH, DK]), ALU.mult)
            dve.drain()
            TT(n_s[:, :], n_s[:, :], n_t[:, :], ALU.add)
            dve.tensor_copy(srows[:, 1024:1032].rearrange("p (c h) -> p c h", c=2), srt[:, 4:6, :])
            TT(srows[:, 1032:1036], R(4), R(11), ALU.mult)
            TT(srows[:, 1036:1040], R(8), R(11), ALU.mult).then_inc(s_srd, 1)
            low(At(S_V + 5))
            with dve.Fori(2, 4) as i:
                for t in range(2):
                    low(At(S_V + t + 2, i, 2))
            evacuated(dve, At(S_V + 7))
            evacuated(dve, At(S_V + 6))
            dve.wait_ge(s_scal, 16)
            bh = lambda a: a.rearrange("p b (h a) -> p b h a", h=NH)
            pairs = lambda r: sc[:, :, r * NH:(r + 1) * NH].unsqueeze(3).broadcast_to([P, NB, NH, 2])
            TT(bh(wvq[:, :, :]), bh(vs[:, :, :]), pairs(3), ALU.mult)
            TT(bh(wv[:, :, :]), bh(vs[:, :, :]), pairs(1), ALU.mult).then_inc(s_cn, 1)

            def o_step(i, t):
                cm, b = c_ring[:, t, :, :], i * 4 + t
                dve.wait_ge(s_cl[t], i * 16 + 16)
                dve.wait_ge(s_tq, b + 1)
                dve.tensor_reduce(hs[:, b, :], tq[t % 2][:, :, :], AX_X, ALU.add)
                dve.wait_ge(s_kv, b + 1)
                for f in range(KT):
                    o = STT(cm[:, f, :], cm[:, f, :], sc[:, b, f // 2:f // 2 + 1], kv[:, f, :], ALU.mult, ALU.add)
                o.then_inc(s_cn, 1)
                low(At(S_O + t + 2, i, 4))

            with dve.Fori(0, 2) as i:
                for t in range(4):
                    o_step(i, t)
            dve.drain()
            TT(bh(hs[:, :, :]), bh(hs[:, :, :]), pairs(2), ALU.mult)
            dve.drain()
            TT(hs[:, :, :], hs[:, :, :], wvq[:, :, :], ALU.add)
            evacuated(dve, At(S_O + 7))
            evacuated(dve, At(S_O + 6))
            dve.drain()
            TT(so[:, :, SEQ:TOK], so[:, :, SEQ:TOK], hs[:, :, :].rearrange("p b f -> p f b"), ALU.mult).then_inc(s_p, 1)
            dve.wait_ge(s_hah, 1)
            TT(hal[:, :, SEQ:TOK], so[:, :, SEQ:TOK], hah[:, :, SEQ:TOK].bitcast(F32), ALU.subtract).then_inc(s_hal, 1)

            with dve.Fori(0, NC) as c:
                for t in range(4):
                    n = At(S_BY + t, c, 4)
                    num, b = trp[t % 2][:, 2, 0:1], t % 2
                    dve.wait_ge(s_num, c * 4 + (t + 1))
                    TS(nd[:, b, 0:1], num, -1.0, None, ALU.mult)
                    dve.drain()
                    STT(nd[:, b, 1:2], num, nd[:, b, 0:1], enm[:, c, t:t + 1], ALU.max, ALU.max)
                    dve.drain()
                    dve.reciprocal(nd[:, b, 2:3], nd[:, b, 1:2]).then_inc(s_rd, 1)
                    dve.wait_ge(s_unit, c * 4 + (t + 1))
                    STT(state[:, t, :], state[:, t, :], decay[:, c, t:t + 1], aux[:, 0, 0:DVA], ALU.mult, ALU.add)\
                        .then_inc(s_st, 1)
                    low(n.plus(2))
                    dve.wait_ge(s_ht, c * 4 + (t + 1))
                    part = (slice(None), slice(2 * t, 2 * t + 2), bass.ds(c * P, P))
                    TT(so[part], so[part], aux[:, 1, 0:DV].rearrange("p (a b) -> p a b", a=2), ALU.mult).then_inc(s_p, 1)
                    if t % 2 == 1:
                        ready(n)
                        evacuated(dve, n.plus(-1))
                        for r in range(4):
                            dve.wait_ge(s_cs[r], 32)
                        TT(both(merged[:, c * 2 + t // 2, :]), both(ftmp[t // 2][:, :]), out2(n), ALU.mult)\
                            .then_inc(evac[n.c % 2], 1)
                    dve.wait_ge(s_hah, c * 4 + (t + 2))
                    TT(hal[part], so[part], hah[part].bitcast(F32), ALU.subtract).then_inc(s_hal, 1)

            with dve.Fori(0, KT) as i:
                n = At(S_AY + 1, i, 2)
                low(n.plus(1))
                ready(n)
                evacuated(dve, n.plus(-1))
                TT(both(ftmp[0][:, :]), both(ftmp[0][:, :]), out2(n), ALU.mult).then_inc(evac[n.c % 2], 1)
                low(n.plus(2))
                dve.drain()
                TT(merged[:, i, :], merged[:, i, :], ftmp[0][:, :], ALU.add).then_inc(s_ms, 1)
                dve.wait_ge(s_mh, i + 1)
                TT(ml[:, i, :], merged[:, i, :], mh[:, i, :].bitcast(F32), ALU.subtract).then_inc(s_m, 1)

            dve.wait_ge(s_xres, 16)
            with dve.Fori(0, KT // 2) as i:
                for t in range(2):
                    n = At(S_WO + t, i, 2)
                    j = i * 2 + t
                    ready(n)
                    TT(both(x1[:, j, :]), out2(n), both(xres[:, j, :]), ALU.add).then_inc(evac[n.c % 2], 1)
                    dve.drain()
                    dve.nop().then_inc(s_x1, 1)
                    low(n.plus(2))
                    dve.wait_ge(s_x2h, i * 2 + (t + 1))
                    STT(x2l[:, j, :], x1[:, j, :], gains[:, 2, bass.ds(j, 1)], x2h[:, j, :].bitcast(F32),
                        ALU.mult, ALU.subtract).then_inc(s_x2, 1)

            def hidden_low(i):
                dve.wait_ge(s_ah, i + 1)
                TT(actl[:, i, :], silu[:, :], acth[:, i, :].bitcast(F32), ALU.subtract).then_inc(s_al, 1)

            def up_step(i, first=False, last=False):
                for t in range(2):
                    n = At(S_UP + t, i, 2)
                    f = i * 2 + t
                    if first and t == 0:
                        dve.memset(up[0][:, 0:2], 0.0)
                        dve.memset(up[1][:, 0:2], 0.0)
                        dve.wait_ge(s_std2, 1)
                        dve.reciprocal(rbc2[:, :], rbc2[:, :])
                        low(n.plus(2))
                        dve.drain()
                    ready(n)
                    if not first:
                        dve.wait_ge(s_nc, i * 2 + (t - 1))
                    TT(both(up[t][:, 2:2 + TOK]), out2(n), both(rbc2[:, :]), ALU.mult).then_inc(evac[n.c % 2], 1)
                    dve.drain()
                    dve.nop().then_inc(s_up, 1)
                    if t == 0 and not first:
                        hidden_low(i - 1)
                    if not (first and t == 0):
                        low(n.plus(2), (DN_CUTS[t + 1] - DN_CUTS[t]) * P if last else KT * P)
                    STT(conv[t][:, SEQ:TOK], up[t][:, 2 + SEQ:2 + TOK], cwb[:, f, 2:3], sconv[:, f, :], ALU.mult, ALU.add)
                    dve.wait_ge(s_tap, i * 2 + (t + 1))
                    STT(conv[t][:, 0:SEQ], up[t][:, 1:1 + SEQ], cwb[:, f, 1:2], conv[t][:, 0:SEQ], ALU.mult, ALU.add)
                    dve.drain()
                    STT(conv[t][:, 0:SEQ], up[t][:, 0:SEQ], cwb[:, f, 0:1], conv[t][:, 0:SEQ], ALU.mult, ALU.add)\
                        .then_inc(s_cv, 1)
                dve.drain()
                dve.wait_ge(s_sil, i + 1)
                TT(silu[:, :], silu[:, :], conv[1][:, :], ALU.mult).then_inc(s_pr, 1)

            dve.wait_ge(s_scv, 1)
            up_step(0, True)
            with dve.Fori(1, FT - 1) as i:
                up_step(i)
            up_step(FT - 1, last=True)
            hidden_low(FT - 1)

            def dn_tile(i, t, final=False):
                for s in range(1 if final else 3):
                    w = (3 * t + s + 2) % 3
                    low(At(S_DN + 3 * t + s + 2, i, 6), (DN_CUTS[w + 1] - DN_CUTS[w]) * P)
                j = i * 2 + t
                dve.wait_ge(done, At(S_DN + 3 * t + 2, i, 6)(2))
                bank = (S_DN + t) % 2
                o = out_ps[bank][:, :, 0:HALF]
                if final:
                    for a in range(2):
                        h = slice(a * HALF, (a + 1) * HALF)
                        TT(x1[:, j, h], o[:, a, :], x1[:, j, h], ALU.add).then_inc(s_x2f, 1)
                    return
                TT(both(x1[:, j, :]), o, both(x1[:, j, :]), ALU.add).then_inc(evac[bank], 1)
                dve.drain()
                dve.nop().then_inc(s_x2f, 1)
                dve.wait_ge(s_sqf, j + 1)
                TT(acc[:, :], acc[:, :], sqa[:, :], ALU.add).then_inc(s_accf, 1)
                dve.drain()

            dve.memset(acc[:, :], 0.0).then_inc(s_accf, 1)
            with dve.Fori(0, KT // 2 - 1) as i:
                for t in range(2):
                    dn_tile(i, t)
            dn_tile(3, 0)
            dn_tile(3, 1, True)
            for a in range(2):
                dve.wait_ge(s_stdf, a + 1)
                h = slice(a * HALF, (a + 1) * HALF)
                dve.reciprocal(rbcf[:, h], rbcf[:, h]).then_inc(s_rf, 1)
                dve.wait_ge(s_xg, 1)
                dve.drain()
                for j in range(Y_DVE):
                    TT(y[:, j, h], xg[:, j, h], rbcf[:, h], ALU.mult).then_inc(s_y, 1)

        @block.gpsimd
        def _(pool):
            pool.memset(ident[:, :], 0.0)
            pool.memset(maskmin[:, :], 0.0)
            pool.drain()
            pool.affine_select(out=ident[:, :], in_=ident[:, :], compare_op=ALU.not_equal, fill=1.0, base=0,
                               pattern=[[-1, P]], channel_multiplier=1)
            pool.affine_select(out=maskmin[:, :], in_=maskmin[:, :], compare_op=ALU.is_ge, fill=BIG, base=0,
                               pattern=[[1, P]], channel_multiplier=-1).then_inc(s_tri, 1)
            pool.memset(g3[:, :], 0.0)
            pool.wait_ge(s_xu, KT)
            pool.wait_ge(s_r1, 1)
            for k in range(KT):
                pool.tensor_tensor(x0[:, k, :], x0[:, k, :], rbc1[:, :], ALU.mult).then_inc(s_xr, 1)
            pool.memset(acct[:, :, :], 0.0).then_inc(s_mp, 1)
            pool.dma_start(ws[:, :, :], ins["w_sT"]).then_inc(s_ws, 16)
            pool.dma_start(gvrow[:, :], ins["g_vrow"].broadcast_to([P, D_MODEL])).then_inc(s_cp, 16)
            pool.dma_start(bs[:, :, :].rearrange("p g t -> p (g t)"), ins["b_s"].broadcast_to([P, NG * P])).then_inc(s_cp, 16)
            pool.dma_start(w00[:, :], ins["w_s00"].broadcast_to([P, NG])).then_inc(s_cp, 16)
            pool.wait_ge(s_ws, 16)
            pool.affine_select(out=ws[:, :, :], in_=ws[:, :, :], compare_op=ALU.is_ge, fill=0.0, base=0,
                               pattern=[[0, NG], [1, P]], channel_multiplier=-1).then_inc(s_tri, 1)

            def squares(jt, t):
                pool.wait_ge(tre[t], jt.half(2))
                g = g_tok[:, :, bass.ds(jt() * P, P)]
                pool.tensor_tensor(sqt[:, :, :], g, g, ALU.mult)
                pool.drain()
                pool.tensor_tensor(acct[:, :, :], acct[:, :, :], sqt[:, :, :], ALU.add)
                pool.drain()

            with pool.Fori(0, 3) as i:
                for t in range(2):
                    squares(At(B_VB + t, i, 2), t)
            pool.wait_ge(tre[0], 5)
            pool.tensor_tensor(sqt[:, :, :], g_tok[:, :, 6 * P:7 * P], g_tok[:, :, 6 * P:7 * P], ALU.mult)
            pool.drain()
            pool.tensor_tensor(acct[:, :, :], acct[:, :, :], sqt[:, :, :], ALU.add)
            pool.wait_ge(tre[1], 5)
            pool.drain()
            pool.tensor_tensor(sqt[:, :, :], g_tok[:, :, 7 * P:8 * P], g_tok[:, :, 7 * P:8 * P], ALU.mult)
            pool.drain()
            pool.tensor_tensor(acct[:, :, :], acct[:, :, :], sqt[:, :, :], ALU.add).then_inc(s_vss, 1)
            pool.wait_ge(s_hbl, 9)
            pool.dma_start(n_s[:, :], ins["n_state"]).then_inc(s_ss, 16)
            pool.dma_start(srt[:, 2, :], ins["m_state"]).then_inc(s_ss, 16)
            pool.dma_start(outs["v_sample"], gvs[:, :, :]).then_inc(s_out, 16)
            pool.wait_ge(s_gcd, 1)
            pool.memset(v_tok[:, :, :, DV:DVA], 1.0)
            pool.dma_start(outs["m_prompt"], mrun[:, NC:NC + 1]).then_inc(s_out, 16)
            pool.wait_ge(s_srd, 1)
            pool.dma_start(scratch, srows[:, :]).then_inc(s_scr, 16)
            pool.dma_start(outs["n_sample"], n_s[:, :]).then_inc(s_nst, 16)
            pool.dma_start(outs["m_sample"], srt[:, 3, :]).then_inc(s_out, 16)
            pool.wait_ge(s_nst, 16)
            pool.wait_ge(s_scr, 16)
            for b in range(NB):
                t = b % 4
                pool.wait_ge(s_bc[t], (b // 4 + 1) * 16)
                pool.wait_ge(s_cl[t], (b // 4 + 1) * 16)
                if b >= 2:
                    pool.wait_ge(s_cn, b)
                pair = lambda a: a.rearrange("p (h a) k -> p h a k", h=NH)
                pool.tensor_tensor(pair(tq[b % 2][:, :, :]), pair(c_ring[:, t, :, :]),
                                   rows[t][:, 512:1024].rearrange("p (h k) -> p h k", h=NH).unsqueeze(2)
                                   .broadcast_to([P, NH, 2, DK]), ALU.mult).then_inc(s_tq, 1)

            pool.wait_ge(s_cn, NB)
            def stage_unit(c, t, first=False):
                if not (first and t < 2):
                    pool.wait_ge(s_unit, c * 4 + (t - 1))
                span = bass.ds(c * P, P) if not isinstance(c, int) else slice(c * P, (c + 1) * P)
                pool.tensor_copy(sds[t % 2][:, :], sd[:, t, c, :])
                pool.tensor_copy(qs[t % 2][:, :], qT[:, t, span])
                pool.tensor_tensor(kw[t % 2][:, :], k_tok[:, c, t, :], wlast[:, c, t:t + 1].broadcast_to([P, P]), ALU.mult)\
                    .then_inc(s_stg, 1)

            for t in range(4):
                stage_unit(0, t, True)
            with pool.Fori(1, NC) as c:
                for t in range(4):
                    stage_unit(c, t)

            pool.wait_ge(s_unit, NC * NH)
            pool.dma_start(xres[:, :, :], ins["x_all"]).then_inc(s_xres, 16)
            pool.wait_ge(s_st, NC * NH + 1)
            pool.dma_start(outs["state"], state[:, :, :]).then_inc(s_out, 16)
            pool.wait_ge(done, S_WO + 1)
            pool.dma_start(cst[:, :, :, :], ins["conv_state"]).then_inc(s_ffl, 16)
            pool.dma_start(cwb[:, :, :], ins["conv_wb"]).then_inc(s_ffl, 16)
            pool.wait_ge(s_ffl, 32)
            pool.dma_start(outs["conv_old"], cst[:, :, 1, :]).then_inc(s_out, 16)
            wb = lambda k: cwb[:, :, k:k + 1].broadcast_to([P, 2 * FT, NB])
            pool.tensor_tensor(sconv[:, :, :], cst[:, :, 0, :], wb(0), ALU.mult)
            pool.tensor_tensor(sct[:, :, :], cst[:, :, 1, :], wb(1), ALU.mult)
            pool.drain()
            pool.tensor_tensor(sconv[:, :, :], sconv[:, :, :], wb(3), ALU.add)
            pool.drain()
            pool.tensor_tensor(sconv[:, :, :], sconv[:, :, :], sct[:, :, :], ALU.add).then_inc(s_scv, 1)
            pool.memset(acc[:, :], 0.0)
            pool.drain()
            for j in range(KT):
                pool.wait_ge(s_x1, j + 1)
                pool.tensor_tensor(sqa[:, :], x1[:, j, :], x1[:, j, :], ALU.mult)
                pool.drain()
                pool.tensor_tensor(acc[:, :], acc[:, :], sqa[:, :], ALU.add)
                pool.drain()
            pool.nop().then_inc(s_acc, 1)

            with pool.Fori(0, FT) as i:
                for t in range(2):
                    pool.wait_ge(s_up, i * 2 + (t + 1))
                    pool.tensor_copy(nconv[:, i * 2 + t, :], up[t][:, SEQ:2 + TOK]).then_inc(s_nc, 1)
            pool.wait_ge(s_nc, 2 * FT)
            pool.dma_start(outs["conv_new"], nconv[:, :, :]).then_inc(s_out, 16)
            for a in range(2):
                h = slice(a * HALF, (a + 1) * HALF)
                pool.wait_ge(s_rf, a + 1)
                for j in range(Y_DVE, KT):
                    pool.wait_ge(s_xg, 1 if j < KT - 1 else 2)
                    pool.tensor_tensor(y[:, j, h], xg[:, j, h], rbcf[:, h], ALU.mult).then_inc(s_yp, 1)
            for t in range(4):
                pool.wait_ge(s_cs[t], 32)
            pool.wait_ge(s_out, 16 * 6)

        @block.tensor
        def _(pe):
            def MM(*a, **k):
                return pe.matmul(*a, **k)

            def tile(n, hi, lo, k0=0, nk=KT, bank=None, use=None, start=True, stop=True, mid=None, mid_at=3, each=None, end=None):
                p = n.c % 2
                pe.wait_ge(w_lo, n(1))
                if start:
                    pe.wait_ge(evac[p if bank is None else bank], n.half(1) if use is None else use)
                o = out_ps[p if bank is None else bank]
                for k in range(nk):
                    if each is not None:
                        pe.wait_ge(each, k + 1)
                    w = slice(k * P, (k + 1) * P)
                    for wt, x in ((whi[p], hi), (whi[p], lo), (wlo[p], hi)):
                        for a in range(2):
                            m = MM(o[:, a, 0:HALF], wt[:, w], x[:, k0 + k, a * HALF:(a + 1) * HALF],
                                   start=start and k == 0 and wt is whi[p] and x is hi,
                                   stop=stop and k == nk - 1 and wt is wlo[p])
                    if k == mid_at and mid is not None:
                        mid()
                m.then_inc(done, 1)
                if end is not None:
                    end()

            def transposes(b, evn):
                evacuated(pe, evn)
                pe.wait_ge(tre[b.c % 2], b.half(1))
                for c in range(NC):
                    m = pe.transpose(trp[b.c % 2][:, c, :], ftmp[b.c % 2][:, c * P:(c + 1) * P], ident[:, :])
                m.then_inc(tr_done, 1)

            pe.wait_ge(evac[0], 1)
            for k in range(KT):
                pe.wait_ge(s_sq[k % 2], k // 2 + 1)
                for a in range(2):
                    m = MM(aux[:, a, 0:HALF], ones[:, :], sq[k % 2][:, a * HALF:(a + 1) * HALF],
                           start=k == 0, stop=k == KT - 1)
                m.then_inc(s_ssk if k < KT - 1 else done, 1)
            def vb_tile(i, t, each=None):
                n = At(S_VB + t, i, 2)
                tile(n, xh, xl, each=each, mid_at=5, mid=lambda: transposes(At(B_VB + t - 1, i, 2), n.plus(-1)))

            tile(At(S_GATE), xuh, xul, each=s_xu)
            tile(At(S_VB), xuh, xul)
            pe.wait_ge(s_tri, 1)
            tile(At(S_VB + 1), xuh, xul, end=lambda: transposes(At(B_VB), At(S_VB)))
            vb_tile(1, 0, each=s_xn)
            vb_tile(1, 1)
            with pe.Fori(2, 4) as i:
                for t in range(2):
                    vb_tile(i, t)

            def v_sums():
                pe.wait_ge(s_ssm, 1)
                MM(aux[:, 1, 80:88], ones[:, :], cq[:, :], start=True, stop=True).then_inc(s_ssk, 1)

            tile(At(S_Q), xh, xl, mid_at=5, mid=lambda: transposes(At(B_VB + 7), At(S_VB + 7)))
            tile(At(S_Q + 1), xh, xl, mid=v_sums)
            for j in range(2, NH):
                tile(At(S_Q + j), xh, xl)

            def spatial(i, t):
                b = At(B_SP + t, i, 2)
                pe.wait_ge(s_vst, i * 2 + (t + 1))
                pe.wait_ge(tre[t], b.half(1))
                for c in range(NC):
                    m = MM(trp[t][:, c, :], vst[t][:, c, :], ws[:, i, :], start=True, stop=True)
                m.then_inc(tr_done, 1)

            def gate_columns():
                pe.wait_ge(s_grow, 1)
                for c in range(NC):
                    pe.transpose(aux[:, 0, c * P:(c + 1) * P], g3[:, c * P:(c + 1) * P], ident[:, :])
                MM(aux[:, 1, 0:32], ones[0:NH, :], dm[:, :, :, :].rearrange("k a c h -> k (a c h)"), start=True, stop=True)
                MM(aux[0:NB, 1, 64:68], ig[:, SEQ:TOK], ident[0:NH, 0:NH], start=True, stop=True)
                MM(aux[0:NB, 1, 68:72], lf[:, SEQ:TOK], ident[0:NH, 0:NH], start=True, stop=True).then_inc(s_gcd, 1)

            pe.wait_ge(s_tri, 2)
            for t in range(2):
                tile(At(S_U + t), xh, xl, end=lambda: spatial(0, t))
            with pe.Fori(1, 4) as i:
                for t in range(2):
                    tile(At(S_U + t, i, 2), xh, xl, end=lambda: spatial(i, t))
            gate_columns()
            def k_side(h):
                evacuated(pe, At(S_K + h))
                if h == 0:
                    pe.wait_ge(s_gcol, 1)
                else:
                    pe.wait_ge(s_auxu, h)
                for c in range(NC):
                    s = slice(c * P, (c + 1) * P)
                    MM(aux[:, 0, s], ftmp[h % 2][:, s], qT[:, h, s], start=True, stop=True)
                MM(aux[:, 1, :], ones[0:NH, :], nmx[:, h, :], start=True, stop=True)
                transposes(At(B_K + h), At(S_K + h))

            for h in range(NH):
                tile(At(S_K + h), xh, xl, mid=(lambda: k_side(h - 1)) if h >= 1 else None)

            def sample_rows():
                pe.wait_ge(s_auxu, NH)
                for h in range(NH):
                    pe.transpose(aux[0:NB, 0, h * P:(h + 1) * P], ks[:, h, :], ident[:, :])
                    m = pe.transpose(aux[0:NB, 1, h * P:(h + 1) * P], qT[:, h, SEQ:TOK], ident[:, :])
                m.then_inc(s_rowd, 1)

            tile(At(S_V), xh, xl, mid=lambda: k_side(NH - 1))
            tile(At(S_V + 1), xh, xl, mid=lambda: transposes(At(B_V), At(S_V)), end=sample_rows)
            with pe.Fori(1, 4) as i:
                for t in range(2):
                    tile(At(S_V + t, i, 2), xh, xl,
                         mid=lambda: transposes(At(B_V + t - 1, i, 2), At(S_V + t - 1, i, 2)))
            tile(At(S_O), xh, xl, mid=lambda: transposes(At(B_V + 7), At(S_V + 7)))
            tile(At(S_O + 1), xh, xl)
            with pe.Fori(1, 4) as i:
                for t in range(2):
                    tile(At(S_O + t, i, 2), xh, xl)

            def unit_products(c, t):
                b = At(B_UNIT + t, c, 4)
                pe.wait_ge(s_stg, c * 4 + (t + 1))
                pe.wait_ge(tre[t % 2], b.half(1))
                pe.wait_ge(s_st, c * 4 + (t + 1))
                num = trp[t % 2][:, :, :].rearrange("p a b -> p (a b)")[:, 0:DVA]
                MM(num, qs[t % 2][:, :], state[:, t, :], start=True, stop=False)
                MM(num, sds[t % 2][:, :], v_tok[:, c, t, :], start=False, stop=True).then_inc(s_num, 1)
                MM(aux[:, 0, 0:DVA], kw[t % 2][:, :], v_tok[:, c, t, :], start=True, stop=True).then_inc(s_unit, 1)

            def unit_transposes(c, t):
                b = At(B_UNIT + t, c, 4)
                pe.wait_ge(tre[t % 2], b.half(2))
                for a in range(2):
                    m = pe.transpose(aux[:, 1, a * P:(a + 1) * P], hn[t % 2][:, a * P:(a + 1) * P], ident[:, :])
                m.then_inc(s_ht, 1)

            pe.wait_ge(s_hbl, 9)
            with pe.Fori(0, NC) as c:
                for t in range(4):
                    xs = (xh, xl) if t % 2 == 0 else (hbh, hbl)
                    tile(At(S_BY + t, c, 4), *xs, mid_at=1, mid=lambda: unit_products(c, t), end=lambda: unit_transposes(c, t))

            with pe.Fori(0, KT) as i:
                tile(At(S_AY, i, 2), xh, xl)
                pe.wait_ge(s_hal, NC * NH + 1)
                tile(At(S_AY + 1, i, 2), hah, hal)

            tile(At(S_WO), mh, ml, each=s_m)
            tile(At(S_WO + 1), mh, ml)
            with pe.Fori(1, 4) as i:
                for t in range(2):
                    tile(At(S_WO + t, i, 2), mh, ml)

            def norm_sums(ready, count, signal):
                pe.wait_ge(ready, count)
                for a in range(2):
                    m = MM(aux[:, a, 0:HALF], ones[:, :], acc[:, a * HALF:(a + 1) * HALF], start=True, stop=True)
                m.then_inc(signal, 1)

            tile(At(S_UP), x2h, x2l, each=s_x2, mid_at=5, mid=lambda: norm_sums(s_acc, 1, s_ss2))
            tile(At(S_UP + 1), x2h, x2l)
            with pe.Fori(1, FT) as i:
                for t in range(2):
                    tile(At(S_UP + t, i, 2), x2h, x2l)

            def dn_pair(i, first=False):
                for s in range(6):
                    t, q = s // 3, s % 3
                    bank = (S_DN + t) % 2
                    n = At(S_DN + s, i, 6)
                    if first and s < 3:
                        pe.wait_ge(s_al, FT - 1 if q < 2 else FT)
                    tile(n, acth, actl, k0=DN_CUTS[q], nk=DN_CUTS[q + 1] - DN_CUTS[q], bank=bank,
                         use=At(S_DN + t, i, 2).half(1), start=q == 0, stop=q == 2)

            dn_pair(0, True)
            with pe.Fori(1, KT // 2) as i:
                dn_pair(i)
            pe.wait_ge(s_accf, KT)
            for a in range(2):
                MM(aux[:, a, 0:HALF], ones[:, :], acc[:, a * HALF:(a + 1) * HALF], start=True, stop=False)
            for a in range(2):
                pe.wait_ge(s_sqf, KT + a)
                MM(aux[:, a, 0:HALF], ones[:, :], sqa[:, a * HALF:(a + 1) * HALF], start=False, stop=True)\
                    .then_inc(s_ssf, 1)


_OUTS = {
    "y": (P, KT, TOK), "state": (P, NH, DVA), "m_prompt": (NH, 1), "conv_new": (P, 2 * FT, 2 + NB),
    "conv_old": (P, 2 * FT, NB), "C_sample": (NB, P, KT, DK), "n_sample": (NB, NH * DK), "m_sample": (NB, NH),
    "v_sample": (P, KT, NB),
}


def kernel(**inputs):
    import numpy as np
    import concourse.bacc as bacc
    from concourse.bass_utils import run_bass_kernel_spmd as run

    a = {k: np.asarray(v) for k, v in inputs.items()}
    w_in = a["w_in"][0]

    def slot(w, c):
        return w[:, c:c + P].reshape(KT, P, P).transpose(1, 0, 2).reshape(P, KT * P)

    hk, hv = NH * DK, NH * DV
    q0, k0, v0, o0 = 0, hk, 2 * hk, 2 * hk + hv
    i0 = o0 + hv
    f0, u0 = i0 + NH, i0 + 2 * NH
    vb0, ga0, gb0 = u0 + D_MODEL, u0 + 2 * D_MODEL, u0 + 3 * D_MODEL
    gates = slot(np.concatenate([w_in[:, i0:i0 + 32], w_in[:, f0:f0 + 96]], axis=1), 0)
    slots = [gates]
    for c0, m in ((vb0, 8), (q0, 4), (u0, 8), (k0, 4), (v0, 8), (o0, 8)):
        slots += [slot(w_in, c0 + j * P) for j in range(m)]
    for j in range(8):
        slots += [slot(w_in, gb0 + j * P), slot(a["w_branch_b"][0], j * P)]
    for j in range(8):
        slots += [slot(w_in, ga0 + j * P), slot(a["w_branch_a"][0], j * P)]
    slots += [slot(a["w_out"][0], j * P) for j in range(8)]
    for j in range(FT):
        slots += [slot(a["w_up"][0], j * P), slot(a["w_up"][0], D_FF + j * P)]
    w_dn = a["w_down"][0].reshape(FT, P, KT, P).transpose(2, 1, 0, 3).reshape(KT, P, FT * P)

    x_all = np.concatenate([a["x_prompt"][0], a["x_sample"][:, 0]], axis=0).T.reshape(KT, P, TOK)
    cols = lambda v: v.reshape(KT, P).T
    order = [f for j in range(FT) for f in (j, FT + j)]
    ff = lambda v: v.reshape(v.shape[:-1] + (2 * FT, P))[..., order, :]
    conv_wb = np.concatenate([ff(a["conv_w"][0]), ff(a["conv_b"])], axis=0).transpose(2, 1, 0)
    arrays = {
        "w_slots": np.stack(slots), "w_dn": w_dn, "x_all": x_all.transpose(1, 0, 2),
        "gains": np.stack([cols(a["g_norm1"][0]), cols(a["g_vnorm"][0]), cols(a["g_norm2"][0]), cols(a["g_final"])], axis=1),
        "gate_b": np.stack([a["b_igate"][0], a["b_fgate"][0]], axis=1),
        "g_vrow": a["g_vnorm"], "b_s": a["b_spatial"].reshape(1, NG * P),
        "w_sT": a["w_spatial"][0].transpose(2, 0, 1), "w_s00": a["w_spatial"][:, :, 0, 0],
        "C_state": a["state_mlstm_C"][0].reshape(NB, NH, 2, P, DK).transpose(0, 3, 1, 2, 4).reshape(NB, P, KT, DK),
        "n_state": a["state_mlstm_n"][0].reshape(NB, NH * DK), "m_state": a["state_mlstm_m"][0],
        "conv_state": ff(a["state_ffn_conv"][0]).transpose(3, 2, 1, 0), "conv_wb": conv_wb,
    }
    nc = bacc.Bacc("TRN2", target_bir_lowering=False, num_devices=1)
    feed, ins, outs = {}, {}, {}
    for name, v in arrays.items():
        v = np.ascontiguousarray(v)
        feed[f"in_{name}"] = v
        ins[name] = nc.dram_tensor(f"in_{name}", v.shape, mybir.dt.from_np(v.dtype), kind="ExternalInput").ap()
    for name, shape in _OUTS.items():
        outs[name] = nc.dram_tensor(f"out_{name}", shape, F32, kind="ExternalOutput").ap()
    hybrid_layer(nc, ins, outs)
    r = run(nc, [feed], core_ids=[0]).results[0]
    r = {name: np.asarray(r[f"out_{name}"]) for name in _OUTS}

    tok = r["y"].transpose(2, 1, 0).reshape(TOK, D_MODEL)
    back = np.argsort(order)
    rows = lambda v: v.transpose(2, 1, 0)[:, back, :].reshape(-1, 2 * D_FF)
    new = rows(r["conv_new"])
    return (
        tok[None, :SEQ], tok[SEQ:, None],
        r["state"][:, :, 0:DV].transpose(1, 2, 0)[None, None], r["state"][:, :, DV].T[None, None],
        r["m_prompt"].reshape(1, 1, NH), new[None, None, 0:2],
        r["C_sample"].reshape(NB, P, NH, 2, DK).transpose(0, 2, 3, 1, 4).reshape(1, NB, NH, DV, DK),
        r["n_sample"].reshape(1, NB, NH, DK), r["m_sample"][None],
        np.stack([rows(r["conv_old"]), new[2:]], axis=1)[None],
        r["v_sample"].transpose(2, 1, 0).reshape(1, NB, 1, D_MODEL),
    )
```
